# Optimizing a Trainium2 kernel written in Bass

```python
import jax
import jax.numpy as jnp
from jax import lax
import numpy as np

D_MODEL = 1024
BATCH = 1
SEQ = 2048
DEPTH = 1
DEC_BATCH = 8
DEC_SEQ = 8
PAST_LEN = 8192
PAGE_SIZE = 128

MIX_WIDTH = D_MODEL
ATTN_WIDTH = MIX_WIDTH // 2
CONV_CH = MIX_WIDTH - ATTN_WIDTH
HEAD_DIM = 64
N_HEADS = ATTN_WIDTH // HEAD_DIM
N_KV_HEADS = 2
Q_PER_KV = N_HEADS // N_KV_HEADS
KV_WIDTH = N_KV_HEADS * HEAD_DIM
WINDOW = 128
ROT_DIM = HEAD_DIM // 4
ROPE_THETA = 500000.0
CONV_K = 3
IN_COLS = ATTN_WIDTH + 2 * KV_WIDTH + 3 * CONV_CH
N_EXPERTS = 64
TOP_K = 6
EXPERT_FF = 256
SHARED_FF = 256
N_EXPERT_GROUPS = 8
TOPK_GROUPS = 4
EXPERTS_PER_GROUP = N_EXPERTS // N_EXPERT_GROUPS
ROUTED_SCALE = 2.5
MOE_BLOCK = 128
LN_EPS = 1e-5
RMS_EPS = 1e-6
ALPHA = (2.0 * DEPTH) ** 0.25
BETA = (8.0 * DEPTH) ** -0.25

kernel_name = 'hybrid_swa_sink_shortconv_moe_deepnorm_step'

def _layer_norm(x, g, b):
    x32 = x.astype(jnp.float32)
    mu = jnp.mean(x32, axis=-1, keepdims=True)
    var = jnp.mean(jnp.square(x32 - mu), axis=-1, keepdims=True)
    y = (x32 - mu) * lax.rsqrt(var + LN_EPS)
    return (y * g.astype(jnp.float32) + b.astype(jnp.float32)).astype(x.dtype)

def _rms_norm(x, g):
    x32 = x.astype(jnp.float32)
    y = x32 * lax.rsqrt(jnp.mean(jnp.square(x32), axis=-1, keepdims=True) + RMS_EPS)
    return (y * g.astype(jnp.float32)).astype(x.dtype)

def _partial_rope(x, pos):
    half = ROT_DIM // 2
    inv_freq = ROPE_THETA ** (-jnp.arange(0, ROT_DIM, 2, dtype=jnp.float32) / ROT_DIM)
    ang = pos.astype(jnp.float32)[:, None] * inv_freq[None, :]
    bshape = (ang.shape[0],) + (1,) * (x.ndim - 3) + (half,)
    cos = jnp.cos(ang).reshape(bshape)
    sin = jnp.sin(ang).reshape(bshape)
    x32 = x.astype(jnp.float32)
    x1 = x32[..., :half]
    x2 = x32[..., half:ROT_DIM]
    out = jnp.concatenate([x1 * cos - x2 * sin, x2 * cos + x1 * sin, x32[..., ROT_DIM:]], axis=-1)
    return out.astype(x.dtype)

def _split_projection(x, w_in):
    B, S, _ = x.shape
    p = x @ w_in
    o1 = ATTN_WIDTH
    o2 = o1 + KV_WIDTH
    o3 = o2 + KV_WIDTH
    o4 = o3 + CONV_CH
    o5 = o4 + CONV_CH
    q = p[..., :o1].reshape(B, S, N_KV_HEADS, Q_PER_KV, HEAD_DIM)
    k = p[..., o1:o2].reshape(B, S, N_KV_HEADS, HEAD_DIM)
    v = p[..., o2:o3].reshape(B, S, N_KV_HEADS, HEAD_DIM)
    u = p[..., o3:o4]
    b_gate = p[..., o4:o5]
    c_gate = p[..., o5:]
    return q, k, v, u, b_gate, c_gate

def _sink_attention(q, k, v, mask, sinks):
    s = jnp.einsum('...qhgd,...khd->...hgqk', q, k).astype(jnp.float32) * (HEAD_DIM ** -0.5)
    s = jnp.where(mask, s, -jnp.inf)
    sink = sinks.astype(jnp.float32)[:, :, None, None]
    m = jnp.maximum(jnp.max(s, axis=-1, keepdims=True), sink)
    p = jnp.exp(s - m)
    denom = jnp.sum(p, axis=-1, keepdims=True) + jnp.exp(sink - m)
    p = (p / denom).astype(v.dtype)
    return jnp.einsum('...hgqk,...khd->...qhgd', p, v)

def _short_conv(u, b_gate, c_gate, conv_w, conv_buf):
    gated = c_gate * u
    ext = jnp.concatenate([conv_buf.astype(gated.dtype), gated], axis=1)
    S = u.shape[1]
    y = conv_w[0] * ext[:, 0:S]
    for tap in range(1, CONV_K):
        y = y + conv_w[tap] * ext[:, tap:tap + S]
    return b_gate * y, ext[:, S:]

def _merge(attn_o, conv_o, g_attn, g_conv, w_out):
    cat = jnp.concatenate([_rms_norm(attn_o, g_attn), _rms_norm(conv_o, g_conv)], axis=-1)
    return cat @ w_out

def _mixer_prompt(x, w_in, sinks, conv_w, g_attn, g_conv, w_out):
    B, S, _ = x.shape
    q, k, v, u, b_gate, c_gate = _split_projection(x, w_in)
    pos = jnp.arange(S)
    q = _partial_rope(q, pos)
    k = _partial_rope(k, pos)
    nb = S // WINDOW
    qb = q.reshape(B, nb, WINDOW, N_KV_HEADS, Q_PER_KV, HEAD_DIM)
    kb = k.reshape(B, nb, WINDOW, N_KV_HEADS, HEAD_DIM)
    vb = v.reshape(B, nb, WINDOW, N_KV_HEADS, HEAD_DIM)

    def with_prev(t):
        prev = jnp.concatenate([jnp.zeros_like(t[:, :1]), t[:, :-1]], axis=1)
        return jnp.concatenate([prev, t], axis=2)

    kk = with_prev(kb)
    vv = with_prev(vb)
    blk = jnp.arange(nb)[:, None] * WINDOW
    qpos = blk + jnp.arange(WINDOW)[None, :]
    kpos = blk - WINDOW + jnp.arange(2 * WINDOW)[None, :]
    diff = qpos[:, :, None] - kpos[:, None, :]
    mask = (diff >= 0) & (diff < WINDOW) & (kpos[:, None, :] >= 0)
    o = _sink_attention(qb, kk, vv, mask[:, None, None], sinks.reshape(N_KV_HEADS, Q_PER_KV))
    o = o.reshape(B, S, ATTN_WIDTH)
    conv_o, conv_state = _short_conv(u, b_gate, c_gate, conv_w, jnp.zeros((B, CONV_K - 1, CONV_CH), x.dtype))
    out = _merge(o, conv_o, g_attn, g_conv, w_out)
    win = min(WINDOW, PAST_LEN)
    return out, k[:, S - win:], v[:, S - win:], conv_state

def _mixer_sample(x, k_buf, v_buf, conv_buf, w_in, sinks, conv_w, g_attn, g_conv, w_out):
    B, S, _ = x.shape
    win = k_buf.shape[1]
    q, k, v, u, b_gate, c_gate = _split_projection(x, w_in)
    pos = PAST_LEN + jnp.arange(S)
    q = _partial_rope(q, pos)
    k = _partial_rope(k, pos)
    kk = jnp.concatenate([k_buf.astype(k.dtype), k], axis=1)
    vv = jnp.concatenate([v_buf.astype(v.dtype), v], axis=1)
    kpos = PAST_LEN - win + jnp.arange(win + S)
    diff = pos[:, None] - kpos[None, :]
    mask = (diff >= 0) & (diff < WINDOW)
    o = _sink_attention(q, kk, vv, mask, sinks.reshape(N_KV_HEADS, Q_PER_KV))
    o = o.reshape(B, S, ATTN_WIDTH)
    conv_o, conv_state = _short_conv(u, b_gate, c_gate, conv_w, conv_buf)
    out = _merge(o, conv_o, g_attn, g_conv, w_out)
    return out, kk[:, S:], vv[:, S:], conv_state

def _route(xt, router_w, router_bias):
    T = xt.shape[0]
    scores = jax.nn.sigmoid((xt @ router_w).astype(jnp.float32))
    sel = scores + router_bias.astype(jnp.float32)
    grp = sel.reshape(T, N_EXPERT_GROUPS, EXPERTS_PER_GROUP)
    gscore = jnp.sum(lax.top_k(grp, 2)[0], axis=-1)
    _, gidx = lax.top_k(gscore, TOPK_GROUPS)
    gmask = jnp.sum(jax.nn.one_hot(gidx, N_EXPERT_GROUPS, dtype=jnp.float32), axis=-2) > 0
    emask = jnp.repeat(gmask, EXPERTS_PER_GROUP, axis=-1)
    _, eidx = lax.top_k(jnp.where(emask, sel, -jnp.inf), TOP_K)
    w = jnp.take_along_axis(scores, eidx, axis=-1)
    w = w / jnp.sum(w, axis=-1, keepdims=True) * ROUTED_SCALE
    return eidx, w

def _routed_experts(xt, eidx, gates, w_gate, w_up, w_down):
    T = xt.shape[0]
    A = T * TOP_K
    n_blocks = -(-A // MOE_BLOCK) + N_EXPERTS
    flat_e = eidx.reshape(A)
    flat_tok = jnp.arange(A, dtype=jnp.int32) // TOP_K
    flat_g = gates.reshape(A).astype(xt.dtype)
    order = jnp.argsort(flat_e)
    sorted_e = flat_e[order]
    counts = jnp.zeros((N_EXPERTS,), jnp.int32).at[flat_e].add(1)
    blocks_per_e = (counts + MOE_BLOCK - 1) // MOE_BLOCK
    block_end = jnp.cumsum(blocks_per_e)
    pad_start = (block_end - blocks_per_e) * MOE_BLOCK
    start = jnp.cumsum(counts) - counts
    rank = jnp.arange(A, dtype=jnp.int32) - start[sorted_e]
    dest = pad_start[sorted_e] + rank
    rows = n_blocks * MOE_BLOCK
    row_tok = jnp.full((rows,), T, jnp.int32).at[dest].set(flat_tok[order])
    row_gate = jnp.zeros((rows,), xt.dtype).at[dest].set(flat_g[order])
    block_expert = jnp.minimum(jnp.searchsorted(block_end, jnp.arange(n_blocks), side='right'), N_EXPERTS - 1)
    xpad = jnp.concatenate([xt, jnp.zeros((1, D_MODEL), xt.dtype)], axis=0)

    def step(acc, blk):
        tok, g, e = blk
        xb = xpad[tok]
        hid = jax.nn.silu(xb @ w_gate[e]) * (xb @ w_up[e])
        yb = (hid @ w_down[e]) * g[:, None]
        return acc.at[tok].add(yb.astype(acc.dtype)), None

    acc0 = jnp.zeros((T + 1, D_MODEL), xt.dtype)
    acc, _ = lax.scan(step, acc0, (row_tok.reshape(n_blocks, MOE_BLOCK), row_gate.reshape(n_blocks, MOE_BLOCK), block_expert))
    return acc[:T]

def _moe(h, router_w, router_bias, w_gate, w_up, w_down, ws_gate, ws_up, ws_down):
    shp = h.shape
    xt = h.reshape(-1, D_MODEL)
    eidx, gates = _route(xt, router_w, router_bias)
    routed = _routed_experts(xt, eidx, gates, w_gate, w_up, w_down)
    shared = (jax.nn.silu(xt @ ws_gate) * (xt @ ws_up)) @ ws_down
    return (routed + shared).reshape(shp)

def setup_inputs(seed: int = 0) -> dict:
    key = jax.random.key(seed)
    ks = jax.random.split(key, 24)

    def nrm(k, shape, scale):
        return jax.random.normal(k, shape, jnp.float32) * scale

    win = min(WINDOW, PAST_LEN)
    v_lo = ATTN_WIDTH + KV_WIDTH
    col_scale = jnp.ones((IN_COLS,), jnp.float32).at[v_lo:v_lo + KV_WIDTH].set(BETA)
    return {
        'x_prompt': nrm(ks[0], (BATCH, SEQ, D_MODEL), 1.0),
        'x_sample': nrm(ks[1], (DEC_BATCH, DEC_SEQ, D_MODEL), 1.0),
        'cache_k': nrm(ks[2], (DEPTH, DEC_BATCH, win, N_KV_HEADS, HEAD_DIM), 1.0),
        'cache_v': nrm(ks[3], (DEPTH, DEC_BATCH, win, N_KV_HEADS, HEAD_DIM), BETA),
        'state_conv': nrm(ks[4], (DEPTH, DEC_BATCH, CONV_K - 1, CONV_CH), 1.0),
        'w_in': nrm(ks[5], (DEPTH, D_MODEL, IN_COLS), D_MODEL ** -0.5) * col_scale,
        'attn_sinks': nrm(ks[6], (DEPTH, N_HEADS), 0.5),
        'conv_w': nrm(ks[7], (DEPTH, CONV_K, CONV_CH), CONV_K ** -0.5),
        'g_attn_out': 1.0 + nrm(ks[8], (DEPTH, ATTN_WIDTH), 0.02),
        'g_conv_out': 1.0 + nrm(ks[9], (DEPTH, CONV_CH), 0.02),
        'w_out': nrm(ks[10], (DEPTH, MIX_WIDTH, D_MODEL), MIX_WIDTH ** -0.5) * BETA,
        'ln1_g': 1.0 + nrm(ks[11], (DEPTH, D_MODEL), 0.02),
        'ln1_b': nrm(ks[12], (DEPTH, D_MODEL), 0.02),
        'router_w': nrm(ks[13], (DEPTH, D_MODEL, N_EXPERTS), D_MODEL ** -0.5),
        'router_bias': nrm(ks[14], (DEPTH, N_EXPERTS), 0.01),
        'w_gate': nrm(ks[15], (DEPTH, N_EXPERTS, D_MODEL, EXPERT_FF), D_MODEL ** -0.5),
        'w_up': nrm(ks[16], (DEPTH, N_EXPERTS, D_MODEL, EXPERT_FF), D_MODEL ** -0.5),
        'w_down': nrm(ks[17], (DEPTH, N_EXPERTS, EXPERT_FF, D_MODEL), EXPERT_FF ** -0.5) * BETA,
        'ws_gate': nrm(ks[18], (DEPTH, D_MODEL, SHARED_FF), D_MODEL ** -0.5),
        'ws_up': nrm(ks[19], (DEPTH, D_MODEL, SHARED_FF), D_MODEL ** -0.5),
        'ws_down': nrm(ks[20], (DEPTH, SHARED_FF, D_MODEL), SHARED_FF ** -0.5) * BETA,
        'ln2_g': 1.0 + nrm(ks[21], (DEPTH, D_MODEL), 0.02),
        'ln2_b': nrm(ks[22], (DEPTH, D_MODEL), 0.02),
    }

def reference(x_prompt, x_sample, cache_k, cache_v, state_conv, w_in, attn_sinks, conv_w, g_attn_out, g_conv_out, w_out, ln1_g, ln1_b, router_w, router_bias, w_gate, w_up, w_down, ws_gate, ws_up, ws_down, ln2_g, ln2_b):
    xp = x_prompt
    xs = x_sample
    kp_l, vp_l, cp_l, ks_l, vs_l, cs_l = [], [], [], [], [], []
    for l in range(DEPTH):
        mp, kp, vp, cp = _mixer_prompt(xp, w_in[l], attn_sinks[l], conv_w[l], g_attn_out[l], g_conv_out[l], w_out[l])
        ms, kn, vn, cn = _mixer_sample(xs, cache_k[l], cache_v[l], state_conv[l], w_in[l], attn_sinks[l], conv_w[l], g_attn_out[l], g_conv_out[l], w_out[l])
        kp_l.append(kp); vp_l.append(vp); cp_l.append(cp)
        ks_l.append(kn); vs_l.append(vn); cs_l.append(cn)
        xp = _layer_norm(ALPHA * xp + mp, ln1_g[l], ln1_b[l])
        xs = _layer_norm(ALPHA * xs + ms, ln1_g[l], ln1_b[l])
        xp = _layer_norm(ALPHA * xp + _moe(xp, router_w[l], router_bias[l], w_gate[l], w_up[l], w_down[l], ws_gate[l], ws_up[l], ws_down[l]), ln2_g[l], ln2_b[l])
        xs = _layer_norm(ALPHA * xs + _moe(xs, router_w[l], router_bias[l], w_gate[l], w_up[l], w_down[l], ws_gate[l], ws_up[l], ws_down[l]), ln2_g[l], ln2_b[l])
    y_prompt = xp
    y_sample = xs
    k_prompt = jnp.stack(kp_l, axis=0)
    v_prompt = jnp.stack(vp_l, axis=0)
    conv_prompt = jnp.stack(cp_l, axis=0)
    k_sample = jnp.stack(ks_l, axis=0)
    v_sample = jnp.stack(vs_l, axis=0)
    conv_sample = jnp.stack(cs_l, axis=0)
    return (y_prompt, y_sample, k_prompt, v_prompt, conv_prompt, k_sample, v_sample, conv_sample)


_drawn_inputs = setup_inputs


def setup_inputs(seed=0):
    import zlib

    import numpy as np

    out = dict(_drawn_inputs(seed))
    spreads = {}
    factors = {'attn_sinks': 4.238, 'ln2_g': 2.749, 'ln2_b': 2.828}
    for name, (base, spread) in spreads.items():
        noise = np.random.default_rng([zlib.crc32(name.encode()), seed]).standard_normal(out[name].shape)
        drawn = base * np.exp(spread * noise) if base else spread * noise
        out[name] = jnp.asarray(drawn.astype(out[name].dtype))
    for name, factor in factors.items():
        out[name] = (out[name] * factor).astype(out[name].dtype)
    return out
```

```python
from contextlib import ExitStack

import numpy as np
import concourse.bass as bass
from concourse import mybir

F32, F32R, BF16 = mybir.dt.float32, mybir.dt.float32r, mybir.dt.bfloat16
I32, U32 = mybir.dt.int32, mybir.dt.uint32
ACT = mybir.ActivationFunctionType
ALU = mybir.AluOpType
AX_X = mybir.AxisListType.X

P = 128
D = 1024
KC = D // P
SEQ, DEC_B, DEC_S, PAST = 2048, 8, 8, 8192
T = SEQ + DEC_B * DEC_S
PT_TILES = SEQ // P
TILES = PT_TILES + 1
TPAD = TILES * P
HEADS, KVH, HD, GQ = 8, 2, 64, 4
AW = HEADS * HD
QKV = AW + 2 * KVH * HD
ROT = HD // 4
CH = 512
CC = CH // P
NE, TOPK, FF = 64, 6, 256
FC = FF // P
NG, EPG, TOPG = 8, 8, 4
ALPHA = 2.0 ** 0.25
LN_EPS, RMS_EPS = 1e-5, 1e-6
NEG = -1.0e30
BIG = 3.0e38
BLK = 2 * P
SLOTS = 9 * BLK
TRASH_SLOT = NE * SLOTS
DROP_SLOT = TRASH_SLOT + BLK
SLOT_ROWS = DROP_SLOT + TOPK * P
ROWS = TPAD + P
OVMAX = 50
OVP = OVMAX // 2


def shape_constants():
    f = np.float32
    inv = (f(500000.0) ** (-np.arange(0, ROT, 2, dtype=f) / f(ROT))).astype(f)
    pos = np.concatenate([np.arange(SEQ), np.tile(PAST + np.arange(DEC_S), DEC_B), np.zeros(TPAD - T)]).astype(f)
    ang = (pos[:, None] * inv[None, :]).astype(f)
    c, s = np.cos(ang).astype(f), np.sin(ang).astype(f)
    rope = np.concatenate([c, c, -s, s], 1).reshape(TILES, P, 2 * ROT)
    r, k = np.arange(P)[:, None], np.arange(2 * P)[None, :]
    diff = r + P - k
    mask = np.where((diff >= 0) & (diff < P), f(0), f(NEG))
    mask0 = np.where(k < P, f(NEG), mask)
    row = np.arange(P)
    rb, rt = row // 32, row % 8
    cols = []
    for b in range(4):
        j = np.arange(P)[None, :]
        d = rt[:, None] + P - j
        cols.append((rb[:, None] == b) & (d >= 0) & (d < P))
    halves = []
    for half in range(2):
        new = [(rb[:, None] + 4 * half == b) & (rt[:, None] >= np.arange(DEC_S)[None, :]) for b in range(DEC_B)]
        halves.append(np.where(np.concatenate(cols + new, 1), f(0), f(NEG)))
    smask = np.stack(halves, 1)
    tok = np.arange(P)[:, None] + P * np.arange(TILES)[None, :]
    valid = (tok < T).astype(f)
    drop_to = DROP_SLOT + 1 + P * np.arange(TOPK)[None, None, :] + np.arange(P)[:, None, None]
    drop = ((1 - valid)[:, :, None] * drop_to).astype(f)
    e = np.arange(NE)
    base = np.broadcast_to(e * SLOTS + 1, (P, NE)).astype(f)
    tri = (np.arange(P)[:, None] < np.arange(P)[None, :]).astype(f)
    thr = np.broadcast_to(BLK * np.arange(1, 9), (NE, 8)).astype(f)
    nidx = np.broadcast_to(np.arange(OVMAX), (NE, OVMAX)).astype(f)
    ecol = np.stack([e, e * SLOTS + BLK - TRASH_SLOT, np.full(NE, BLK)], 1).astype(f)
    table0 = np.zeros((DROP_SLOT, 2), np.int32)
    table0[:, 0] = TPAD + np.arange(DROP_SLOT) % P
    return {
        "rope": rope.astype(f), "mask": np.stack([mask0, mask], 1).astype(f), "smask": smask.astype(f),
        "valid": valid, "drop": drop, "tokid": tok.astype(np.int32), "base": base.copy(),
        "tri": tri, "thr": thr.copy(), "nidx": nidx.copy(), "ecol": ecol,
        "table0": table0, "ident": np.eye(P, dtype=f),
    }


def hold(eng, sem, value, passed):
    eng.wait_ge(sem, value)
    eng.sem_inc(passed, 1)


class Phase:

    def __init__(self, nc, ctx, name):
        self.nc, self.ctx, self.name = nc, ctx, name

    def sb(self, name, shape, dt=F32):
        return self.ctx.enter_context(self.nc.sbuf_tensor(f"{self.name}_{name}", shape, dt))

    def ps(self, name, shape, dt=F32):
        return self.ctx.enter_context(self.nc.psum_tensor(f"{self.name}_{name}", shape, dt))

    def sem(self, name):
        return self.ctx.enter_context(self.nc.semaphore(f"{self.name}_{name}"))


def split_weights(nc, ph, pieces, raw):
    loaded = [ph.sem(f"wraw{b}") for b in range(2)]
    rounded, split = ph.sem("whi"), ph.sem("wlo")

    def raw_of(n):
        a, b = pieces[n][1].shape[1:]
        return raw[:, n % 2, 0:a * b].rearrange("p (a b) -> p a b", a=a)

    def sp_part(sp):
        for n, (src, hi, lo) in enumerate(pieces):
            if n >= 2:
                sp.wait_ge(split, n - 1)
            sp.dma_start(raw_of(n), src).then_inc(loaded[n % 2], 16)

    def act_part(act):
        for n, (src, hi, lo) in enumerate(pieces):
            act.wait_ge(loaded[n % 2], 16 * (n // 2 + 1))
            nc.scalar.activation(hi, raw_of(n), ACT.Copy).then_inc(rounded, 1)

    def dve_part(dve):
        for n, (src, hi, lo) in enumerate(pieces):
            dve.wait_ge(rounded, n + 1)
            nc.vector.tensor_tensor(lo, raw_of(n), hi.bitcast(F32), ALU.subtract).then_inc(split, 1)

    return sp_part, act_part, dve_part, split, len(pieces)


SK = 4 * P + DEC_B * DEC_S
NSAMP = DEC_B * DEC_S


def stage_attention(nc, io):
    with ExitStack() as ctx:
        ph = Phase(nc, ctx, "at")
        sb, ps, sem = ph.sb, ph.ps, ph.sem
        wh, wl = sb("wh", [P, KC, QKV], F32R), sb("wl", [P, KC, QKV], F32R)
        wraw = sb("wraw", [P, 2, QKV])
        xr = sb("xr", [P, KC, P])
        xh, xl = sb("xh", [P, KC, P], F32R), sb("xl", [P, KC, P], F32R)
        ident, ones = sb("ident", [P, P]), sb("ones", [P, 2])
        rope, mask = sb("rope", [P, 2 * ROT]), sb("mask", [P, 2, 2 * P])
        sinks, gat = sb("sinks", [P, HEADS]), sb("gat", [P, GQ])
        qk = sb("qk", [P, 10, HD])
        ra, rb = sb("ra", [P, 10, ROT]), sb("rb", [P, 10, ROT])
        qT = sb("qT", [P, GQ, P])
        kT = sb("kT", [P, 2 * P])
        vv = sb("vv", [P, 3, P])
        pr = sb("pr", [P, HEADS, 2 * P])
        pT = sb("pT", [P, KVH, 2, GQ, P])
        mx, ng = sb("mx", [P, HEADS]), sb("ng", [P, HEADS])
        dn, sk, rd = sb("dn", [P, HEADS]), sb("sk", [P, HEADS]), sb("rd", [P, HEADS])
        sq, cat = sb("sq", [P, GQ, P]), sb("cat", [P, GQ, P])
        ssa = sb("ssa", [P, TILES + 1])
        kcT = sb("kcT", [P, 2, SK])
        vc = sb("vc", [P, DEC_B, P])
        sm = sb("sm", [P, 2, SK])
        srow = sb("srow", [P, 4])
        spr = sb("spr", [P, 4, SK])
        spT = sb("spT", [P, 5, P])
        qTs = sb("qTs", [P, 2, P])

        psP = ps("psP", [P, 2, 512])
        psS = ps("psS", [P, HEADS, 2 * P])
        psT, psO = ps("psT", [P, 512]), ps("psO", [P, 512])

        s_const, s_zero, s_passed = sem("const"), sem("zero"), sem("passed")
        s_x, s_xh, s_xl, s_tab = sem("x_loaded"), sem("x_hi"), sem("x_lo"), sem("rope_loaded")
        s_proj, s_copied, s_rope = sem("projected"), sem("qkv_copied"), sem("roped")
        s_qkt, s_qkT = sem("qk_transposed"), sem("qkT_copied")
        s_score, s_max, s_exp, s_rd, s_prob = sem("scores"), sem("maxed"), sem("exped"), sem("rden"), sem("probs")
        s_pT, s_pTa, s_pTd = sem("probsT"), sem("probsT_act"), sem("probsT_dve")
        s_pv, s_sq, s_cat, s_ss, s_sse = sem("pv"), sem("squared"), sem("cat"), sem("sumsq"), sem("sumsq_saved")
        s_st, s_shift, s_kvst = sem("stored"), sem("shifted"), sem("kv_stored")
        s_tail = sem("tail_out")
        s_g, s_ga, s_gp = sem("group_T"), sem("group_copied"), sem("group_pv")
        pieces = [(io["w_in"][:, kc:kc + 1, 0:QKV], wh[:, kc:kc + 1, :], wl[:, kc:kc + 1, :]) for kc in range(KC)]
        w_sp, w_act, w_dve, s_w, n_w = split_weights(nc, ph, pieces, wraw)
        consts = [(ident[:], io["ident"]), (mask[:], io["mask"]), (sm[:], io["smask"]),
                  (sinks[:], io["sinks"].partition_broadcast(P)), (gat[:], io["g_attn"]),
                  (srow[:], io["srow"]), (vc[:], io["cache_v"]),
                  (kcT[:, 0, 0:4 * P], io["cache_kT"][:, 0]), (kcT[:, 1, 0:4 * P], io["cache_kT"][:, 1])]
        CONST = 16 * len(consts)
        block = ctx.enter_context(nc.Block())

        @block.sync
        def _(sp):
            sp.dma_start(xr[:], io["xT"][0]).then_inc(s_x, 16)
            sp.dma_start(rope[:], io["rope"][0]).then_inc(s_tab, 16)
            w_sp(sp)
            for dst, src in consts:
                sp.dma_start(dst, src).then_inc(s_const, 16)

            def stores(i, load_next):
                if load_next:
                    sp.wait_ge(s_xl, i + 1)
                    sp.dma_start(xr[:], io["xT"][bass.ds(i + 1, 1)].rearrange("o p k t -> (o p) k t")).then_inc(s_x, 16)
                sp.wait_ge(s_rope, i + 1)
                if load_next:
                    sp.dma_start(rope[:], io["rope"][bass.ds(i + 1, 1)].rearrange("o p c -> (o p) c")).then_inc(s_tab, 16)
                sp.dma_start(io["kv_all"][bass.ds(i, 1), :, 0].rearrange("o p c -> (o p) c"),
                             qk[:, 8:10, :].rearrange("p h d -> p (h d)")).then_inc(s_kvst, 16)
                sp.dma_start(io["kv_all"][bass.ds(i, 1), :, 1].rearrange("o p c -> (o p) c"),
                             vv[:, 2, :]).then_inc(s_kvst, 16)
                sp.wait_ge(s_cat, i + 1)
                sp.dma_start(io["catA"][bass.ds(i, 1)].rearrange("o p k t -> (o p) k t"), cat[:]).then_inc(s_st, 16)

            with sp.Fori(0, PT_TILES) as i:
                stores(i, True)
            stores(PT_TILES, False)
            sp.wait_ge(s_cat, TILES + 1)
            sp.dma_start(io["catA"][TILES], cat[:]).then_inc(s_st, 16)
            sp.wait_ge(s_sse, TILES + 1)
            sp.dma_start(io["ssA"], ssa[:]).then_inc(s_st, 16)
            sp.wait_ge(s_st, 16 * (TILES + 2))
            sp.wait_ge(s_kvst, 32 * TILES)

        @block.gpsimd
        def _(pool):
            for buf in (pr, kT, ones, vv):
                nc.gpsimd.memset(buf[:], 1.0 if buf is ones else 0.0).then_inc(s_zero, 1)
            pool.dma_start(io["ck_tail"], io["cache_k"][:, DEC_S:]).then_inc(s_tail, 16)
            pool.dma_start(io["cv_tail"], io["cache_vn"][:, DEC_S:]).then_inc(s_tail, 16)
            pool.wait_ge(s_zero, 4)

            def shift(i):
                hold(pool, s_pv, i, s_passed)
                hold(pool, s_kvst, 32 * i, s_passed)
                nc.gpsimd.tensor_copy(vv[:, 0, :], vv[:, 1, :])
                pool.drain()
                nc.gpsimd.tensor_copy(vv[:, 1, :], vv[:, 2, :])
                hold(pool, s_score, i, s_passed)
                nc.gpsimd.tensor_copy(kT[:, 0:P], kT[:, P:2 * P])
                pool.drain().then_inc(s_shift, 1)

            with pool.Fori(0, PT_TILES) as i:
                shift(i)
                pool.wait_ge(s_rd, i + 1)
                nc.gpsimd.tensor_tensor(pr[:], pr[:], rd[:].unsqueeze(2).to_broadcast([P, HEADS, 2 * P]),
                                        ALU.mult).then_inc(s_prob, 1)
            shift(PT_TILES)
            pool.wait_ge(s_rd, TILES)
            nc.gpsimd.tensor_tensor(spr[:], spr[:], rd[:, 0:4].unsqueeze(2).to_broadcast([P, 4, SK]),
                                    ALU.mult).then_inc(s_prob, 1)
            pool.wait_ge(s_tail, 32)

        @block.scalar
        def _(act):
            act.wait_ge(s_x, 16)
            nc.scalar.activation(xh[:], xr[:], ACT.Copy).then_inc(s_xh, 1)
            w_act(act)
            act.wait_ge(s_const, CONST)
            act.wait_ge(s_zero, 4)

            def projected(i):
                act.wait_ge(s_proj, i + 1)
                act.wait_ge(s_shift, i + 1)
                act.wait_ge(s_kvst, 32 * i)
                act.wait_ge(s_qkt, i)
                for kv in range(KVH):
                    nc.scalar.activation(qk[:, kv:8:2, :], psP[:, 0, kv * 256:(kv + 1) * 256].rearrange("p (g d) -> p g d", g=GQ), ACT.Copy)
                nc.scalar.activation(qk[:, 8:10, :].rearrange("p h d -> p (h d)"), psP[:, 1, 0:P], ACT.Copy)
                nc.scalar.activation(vv[:, 2, :], psP[:, 1, P:2 * P], ACT.Copy).then_inc(s_copied, 1)
                act.wait_ge(s_pT, i + 1)
                act.wait_ge(s_pv, i)
                nc.scalar.activation(pT[:, 0].rearrange("p h g q -> p (h g q)"),
                                     psS[:, 0:4].rearrange("p h q -> p (h q)"), ACT.Copy).then_inc(s_pTa, 1)
                act.wait_ge(s_qkt, i + 1)
                act.wait_ge(s_score, i)
                nc.scalar.activation(qT[:].rearrange("p g q -> p (g q)"), psT[:], ACT.Copy)
                nc.scalar.activation(kT[:, P:2 * P], psP[:, 1, 256:384], ACT.Copy).then_inc(s_qkT, 1)

            def squares(n):
                act.wait_ge(s_pv, n + 1)
                act.wait_ge(s_ss, n)
                nc.scalar.activation(sq[:].rearrange("p g q -> p (g q)"), psO[:], ACT.Square).then_inc(s_sq, 1)

            def save(n):
                act.wait_ge(s_ss, n + 1)
                nc.scalar.activation(ssa[:, bass.ds(n, 1)], psP[:, 1, 384:385], ACT.Copy).then_inc(s_sse, 1)

            with act.Fori(0, PT_TILES) as i:
                projected(i)
                act.wait_ge(s_x, 16 * (i + 2))
                nc.scalar.activation(xh[:], xr[:], ACT.Copy).then_inc(s_xh, 1)
                squares(i)
                save(i)
                act.wait_ge(s_max, i + 1)
                for h in range(HEADS):
                    nc.scalar.activation(pr[:, h, :], pr[:, h, :], ACT.Exp, bias=ng[:, h:h + 1],
                                         accum_out=dn[:, h:h + 1])
                nc.scalar.activation(sk[:], sk[:], ACT.Exp).then_inc(s_exp, 1)
            projected(PT_TILES)
            squares(PT_TILES)
            act.wait_ge(s_qkT, TILES)
            for half in range(2):
                for g in range(GQ):
                    nc.scalar.activation(qTs[:, half].rearrange("p (b g t) -> p g b t", b=4, g=GQ)[:, g],
                                         qT[:, g, half * 32:half * 32 + 32].rearrange("p (b t) -> p b t", b=4), ACT.Copy)
                nc.scalar.activation(kcT[:, half, 4 * P:SK], kT[:, P:P + NSAMP], ACT.Copy)
            act.drain().then_inc(s_ga, 1)
            act.wait_ge(s_max, TILES)
            for n in range(4):
                nc.scalar.activation(spr[:, n, :], spr[:, n, :], ACT.Exp, bias=ng[:, n:n + 1],
                                     accum_out=dn[:, n:n + 1])
            nc.scalar.activation(sk[:, 0:4], sk[:, 0:4], ACT.Exp).then_inc(s_exp, 1)
            save(PT_TILES)
            for n in range(4):
                act.wait_ge(s_g, n + 1)
                nc.scalar.activation(spT[:, 0:4, :].rearrange("p b r -> p (b r)"), psT[:], ACT.Copy)
                nc.scalar.activation(spT[0:NSAMP, 4, :], psS[0:NSAMP, 0, 0:P], ACT.Copy).then_inc(s_ga, 1)
            act.wait_ge(s_gp, 4)
            act.wait_ge(s_ss, TILES)
            for half in range(2):
                last = nc.scalar.activation(sq[:, half].rearrange("p (g b t) -> p b g t", b=4, g=GQ),
                                            psO[:, half * P:(half + 1) * P].rearrange("p (b g t) -> p b g t", b=4, g=GQ), ACT.Square)
            last.then_inc(s_sq, 1)
            save(TILES)

        @block.vector
        def _(dve):
            dve.wait_ge(s_xh, 1)
            nc.vector.tensor_tensor(xl[:], xr[:], xh[:].bitcast(F32), ALU.subtract).then_inc(s_xl, 1)
            w_dve(dve)
            nc.vector.memset(cat[:], 0.0)
            nc.vector.memset(ssa[:], 0.0)
            dve.wait_ge(s_const, CONST)
            dve.wait_ge(s_zero, 4)

            def rotate(i):
                dve.wait_ge(s_copied, i + 1)
                dve.wait_ge(s_tab, 16 * (i + 1))
                nc.vector.tensor_tensor(ra[:], qk[:, :, 0:ROT], rope[:, 0:ROT].unsqueeze(1).to_broadcast([P, 10, ROT]), ALU.mult)
                nc.vector.tensor_tensor(rb[:, :, 0:8], qk[:, :, 8:16], rope[:, ROT:ROT + 8].unsqueeze(1).to_broadcast([P, 10, 8]), ALU.mult)
                nc.vector.tensor_tensor(rb[:, :, 8:16], qk[:, :, 0:8], rope[:, ROT + 8:2 * ROT].unsqueeze(1).to_broadcast([P, 10, 8]), ALU.mult)
                dve.drain()
                nc.vector.tensor_tensor(qk[:, :, 0:ROT], ra[:], rb[:], ALU.add).then_inc(s_rope, 1)
                dve.wait_ge(s_pT, i + 1)
                dve.wait_ge(s_pv, i)
                nc.vector.tensor_copy(pT[:, 1].rearrange("p h g q -> p (h g q)"),
                                      psS[:, 4:8].rearrange("p h q -> p (h q)")).then_inc(s_pTd, 1)

            def features(n):
                dve.wait_ge(s_sq, n + 1)
                dve.wait_ge(s_st, 16 * n)
                nc.vector.tensor_tensor(cat[:], psO[:].rearrange("p (g q) -> p g q", g=GQ),
                                        gat[:].unsqueeze(2).to_broadcast([P, GQ, P]), ALU.mult).then_inc(s_cat, 1)

            def softmax_max(i, view, width, snk):
                dve.drain()
                nc.vector.tensor_reduce(mx[:, 0:width], view, AX_X, ALU.max)
                dve.drain()
                nc.vector.tensor_tensor(mx[:, 0:width], mx[:, 0:width], snk, ALU.max)
                dve.drain()
                nc.vector.tensor_scalar(ng[:, 0:width], mx[:, 0:width], -1.0, None, ALU.mult)
                nc.vector.tensor_tensor(sk[:, 0:width], snk, mx[:, 0:width], ALU.subtract)
                dve.drain().then_inc(s_max, 1)
                dve.wait_ge(s_exp, i + 1)
                nc.vector.tensor_tensor(dn[:, 0:width], dn[:, 0:width], sk[:, 0:width], ALU.add)
                dve.drain()
                nc.vector.reciprocal(rd[:, 0:width], dn[:, 0:width]).then_inc(s_rd, 1)

            with dve.Fori(0, PT_TILES) as i:
                rotate(i)
                dve.wait_ge(s_xh, i + 2)
                dve.wait_ge(s_proj, i + 1)
                nc.vector.tensor_tensor(xl[:], xr[:], xh[:].bitcast(F32), ALU.subtract).then_inc(s_xl, 1)
                features(i)
                dve.wait_ge(s_score, i + 1)
                dve.wait_ge(s_pT, i + 1)
                for b in range(4):
                    nc.vector.scalar_tensor_tensor(pr[:, 2 * b:2 * b + 2, :], psS[:, 2 * b:2 * b + 2, :], HD ** -0.5,
                                                   mask[:, 0, :].unsqueeze(1).to_broadcast([P, 2, 2 * P]),
                                                   ALU.mult, ALU.add)
                softmax_max(i, pr[:], HEADS, sinks[:])
                nc.vector.tensor_copy(mask[:, 0, :], mask[:, 1, :])
            rotate(PT_TILES)
            features(PT_TILES)
            dve.wait_ge(s_score, TILES)
            for n in range(4):
                half, new = n % 2, psT if n < 2 else psP[:, 0]
                nc.vector.scalar_tensor_tensor(spr[:, n, 0:4 * P], psS[:, 2 * n:2 * n + 2].rearrange("p h q -> p (h q)"),
                                               HD ** -0.5, sm[:, half, 0:4 * P], ALU.mult, ALU.add)
                nc.vector.scalar_tensor_tensor(spr[:, n, 4 * P:SK], new[:, half * NSAMP:(half + 1) * NSAMP],
                                               HD ** -0.5, sm[:, half, 4 * P:SK], ALU.mult, ALU.add)
            softmax_max(PT_TILES, spr[:], 4, srow[:])
            dve.wait_ge(s_sq, TILES + 1)
            dve.wait_ge(s_st, 16 * TILES)
            nc.vector.memset(cat[:, :, NSAMP:P], 0.0)
            for half in range(2):
                for g in range(GQ):
                    nc.vector.tensor_scalar(cat[:, g, half * 32:half * 32 + 32].rearrange("p (b t) -> p b t", b=4),
                                            psO[:, half * P:(half + 1) * P].rearrange("p (b g t) -> p g b t", b=4, g=GQ)[:, g],
                                            gat[:, g:g + 1], None, ALU.mult)
            dve.drain().then_inc(s_cat, 1)

        @block.tensor
        def _(pe):
            pe.wait_ge(s_w, n_w)
            pe.wait_ge(s_zero, 4)
            pe.wait_ge(s_const, CONST)

            def project(i):
                pe.wait_ge(s_xl, i + 1)
                pe.wait_ge(s_copied, i)
                pe.wait_ge(s_qkT, i)
                pe.wait_ge(s_sse, i)
                passes = [(kc, a, b) for kc in range(KC) for a, b in ((xh, wh), (xh, wl), (xl, wh))]
                for n, (kc, a, b) in enumerate(passes):
                    for j, (lo, hi) in enumerate(((0, 512), (512, QKV))):
                        last = nc.tensor.matmul(psP[:, j, 0:hi - lo], a[:, kc, :], b[:, kc, lo:hi],
                                                start=(n == 0), stop=(n == len(passes) - 1))
                last.then_inc(s_proj, 1)
                pe.wait_ge(s_prob, i)
                for kv in range(KVH):
                    for half in range(2):
                        for g in range(GQ):
                            last = nc.tensor.transpose(
                                psS[:, 4 * kv + 2 * half + g // 2, (g % 2) * P:(g % 2 + 1) * P],
                                pr[:, 4 * kv + g, half * P:(half + 1) * P], ident[:])
                last.then_inc(s_pT, 1)
                pe.wait_ge(s_rope, i + 1)
                for g in range(GQ):
                    nc.tensor.transpose(psT[:, g * P:(g + 1) * P],
                                        qk[:, 2 * g:2 * g + 2, :].rearrange("p h d -> p (h d)"), ident[:])
                nc.tensor.transpose(psP[:, 1, 256:384], qk[:, 8:10, :].rearrange("p h d -> p (h d)"),
                                    ident[:]).then_inc(s_qkt, 1)

            def values(n):
                pe.wait_ge(s_pTa, n + 1)
                pe.wait_ge(s_pTd, n + 1)
                pe.wait_ge(s_cat, n)
                pe.wait_ge(s_sq, n)
                pe.wait_ge(s_shift, n + 1)
                for kv in range(KVH):
                    for half in range(2):
                        last = nc.tensor.matmul(psO[kv * HD:(kv + 1) * HD, :], vv[:, half, kv * HD:(kv + 1) * HD],
                                                pT[:, kv, half].rearrange("p g q -> p (g q)"),
                                                start=(half == 0), stop=(half == 1))
                last.then_inc(s_pv, 1)

            def sum_squares(n, lhs):
                pe.wait_ge(s_sq, n + 1)
                pe.wait_ge(s_sse, n)
                for j, l in enumerate(lhs):
                    last = nc.tensor.matmul(psP[:, 1, 384:385], l, ones[:, 0:1], start=(j == 0), stop=(j == len(lhs) - 1))
                last.then_inc(s_ss, 1)

            with pe.Fori(0, PT_TILES) as i:
                project(i)
                values(i)
                pe.wait_ge(s_qkT, i + 1)
                for h in range(HEADS):
                    kv, g = h // GQ, h % GQ
                    last = nc.tensor.matmul(psS[:, h, :], qT[kv * HD:(kv + 1) * HD, g, :], kT[kv * HD:(kv + 1) * HD, :],
                                            start=True, stop=True)
                last.then_inc(s_score, 1)
                sum_squares(i, [sq[:, g, :] for g in range(GQ)])
            project(PT_TILES)
            values(PT_TILES)
            sum_squares(PT_TILES, [sq[:, g, :] for g in range(GQ)])
            pe.wait_ge(s_ga, 1)
            for n in range(4):
                kv, half = n // 2, n % 2
                lhs = qTs[kv * HD:(kv + 1) * HD, half, :]
                nc.tensor.matmul(psS[:, 2 * n:2 * n + 2].rearrange("p h q -> p (h q)"), lhs,
                                 kcT[kv * HD:(kv + 1) * HD, half, 0:4 * P], start=True, stop=True)
                new = psT if kv == 0 else psP[:, 0]
                last = nc.tensor.matmul(new[:, half * NSAMP:(half + 1) * NSAMP], lhs,
                                        kcT[kv * HD:(kv + 1) * HD, half, 4 * P:SK], start=True, stop=True)
            last.then_inc(s_score, 1)
            pe.wait_ge(s_prob, TILES)
            pe.wait_ge(s_cat, TILES)
            pe.wait_ge(s_sq, TILES)
            for n in range(4):
                kv, half = n // 2, n % 2
                pe.wait_ge(s_ga, n + 1)
                for b in range(4):
                    nc.tensor.transpose(psT[:, b * P:(b + 1) * P], spr[:, n, b * P:(b + 1) * P], ident[:])
                nc.tensor.transpose(psS[0:NSAMP, 0, 0:P], spr[:, n, 4 * P:SK], ident[:]).then_inc(s_g, 1)
                pe.wait_ge(s_ga, n + 2)
                out = psO[kv * HD:(kv + 1) * HD, half * P:(half + 1) * P]
                for b in range(4):
                    nc.tensor.matmul(out, vc[:, 4 * half + b, kv * HD:(kv + 1) * HD], spT[:, b, :],
                                     start=(b == 0), stop=False)
                nc.tensor.matmul(out, vv[0:NSAMP, 2, kv * HD:(kv + 1) * HD], spT[0:NSAMP, 4, :],
                                 start=False, stop=True).then_inc(s_gp, 1)
            pe.wait_ge(s_sq, TILES + 1)
            pe.wait_ge(s_sse, TILES)
            for half in range(2):
                for g in range(GQ):
                    last = nc.tensor.matmul(psP[half * 32:half * 32 + 32, 1, 384:385],
                                            sq[:, half, g * 32:(g + 1) * 32],
                                            ones[:, 0:1], start=(g == 0), stop=(g == GQ - 1))
            last.then_inc(s_ss, 1)


def stage_conv(nc, io):
    N = 4 * P
    STEPS = SEQ // N
    with ExitStack() as ctx:
        ph = Phase(nc, ctx, "cv")
        sb, ps, sem = ph.sb, ph.ps, ph.sem
        wh, wl = sb("wh", [P, KC, 3 * CH], F32R), sb("wl", [P, KC, 3 * CH], F32R)
        xr = sb("xr", [P, 4, KC, P])
        xh, xl = sb("xh", [P, KC, N], F32R), sb("xl", [P, KC, N], F32R)
        gated = sb("gated", [P, CC, N + 2])
        gs = sb("gs", [P, CC, DEC_B, DEC_S + 2])
        us, tmp = sb("us", [P, N]), sb("tmp", [P, N])
        sq, cat = sb("sq", [P, CC, N]), sb("cat", [P, 4, CC, P])
        ones, cw, gcv = sb("ones", [P, 2]), sb("cw", [P, CC, 3]), sb("gcv", [P, CC])
        ssc = sb("ssc", [P, TILES])
        psG = ps("psG", [P, 2, 3, 512])
        psQ = ps("psQ", [P, 512])

        s_const, s_x, s_xh, s_xl = sem("const"), sem("x_loaded"), sem("x_hi"), sem("x_lo")
        s_proj, s_u, s_gate, s_tap, s_conv, s_free = (sem(n) for n in ("projected", "u_copied", "gated", "tap0", "conv", "psum_read"))
        s_sq, s_cat, s_ss, s_sse, s_st, s_zero = (sem(n) for n in ("squared", "cat", "sumsq", "sumsq_saved", "stored", "zero"))
        raw = xr[:].rearrange("p a k t -> p (a k t)")[:, 0:2 * 3 * CH].rearrange("p (b n) -> p b n", b=2)
        pieces = [(io["w_in"][:, kc:kc + 1, QKV:QKV + 3 * CH], wh[:, kc:kc + 1, :], wl[:, kc:kc + 1, :]) for kc in range(KC)]
        w_sp, w_act, w_dve, s_w, n_w = split_weights(nc, ph, pieces, raw)
        block = ctx.enter_context(nc.Block())

        @block.sync
        def _(sp):
            w_sp(sp)
            sp.dma_start(cw[:], io["conv_w"]).then_inc(s_const, 16)
            sp.dma_start(gcv[:], io["g_conv"]).then_inc(s_const, 16)
            sp.dma_start(gs[:, :, :, 0:2], io["state_conv"]).then_inc(s_const, 16)
            sp.wait_ge(s_w, n_w)
            sp.wait_ge(s_zero, 1)

            with sp.Fori(0, STEPS) as i:
                sp.wait_ge(s_xl, i)
                sp.dma_start(xr[:], io["xT"][bass.ds(4 * i, 4)].rearrange("a p k t -> p a k t")).then_inc(s_x, 16)
                sp.wait_ge(s_cat, CC * i)
                sp.dma_start(io["catC"][bass.ds(4 * i, 4)].rearrange("a p k t -> p a k t"), cat[:]).then_inc(s_st, 16)
            sp.wait_ge(s_xl, STEPS)
            sp.dma_start(xr[:, 0], io["xT"][PT_TILES]).then_inc(s_x, 16)
            sp.wait_ge(s_cat, CC * STEPS)
            sp.dma_start(io["catC"][bass.ds(4 * STEPS, 4)].rearrange("a p k t -> p a k t"), cat[:]).then_inc(s_st, 16)
            with nc.allow_non_contiguous_dma(reason="two columns of the state"):
                sp.wait_ge(s_cat, CC * (STEPS + 1))
                sp.dma_start(io["conv_p"], gated[:, :, 0:2]).then_inc(s_st, 16)
                sp.dma_start(io["conv_s"], gs[:, :, :, DEC_S:DEC_S + 2]).then_inc(s_st, 16)
            sp.dma_start(io["catC"][4 + PT_TILES], cat[:, 0]).then_inc(s_st, 16)
            sp.wait_ge(s_sse, STEPS + 1)
            sp.dma_start(io["ssC"], ssc[:]).then_inc(s_st, 16)
            sp.wait_ge(s_st, 16 * (STEPS + 5))

        @block.scalar
        def _(act):
            w_act(act)
            act.wait_ge(s_const, 48)

            def round_x(i, dst, src):
                act.wait_ge(s_x, 16 * (i + 1))
                act.wait_ge(s_proj, 3 * CC * i)
                nc.scalar.activation(dst, src, ACT.Copy).then_inc(s_xh, 1)

            def chunk(m, c, n, g, grid, out):
                act.wait_ge(s_proj, 3 * m + 1)
                act.wait_ge(s_gate, m)
                nc.scalar.activation(us[:, 0:n], psG[:, c % 2, 0, 0:n], ACT.Copy).then_inc(s_u, 1)
                act.wait_ge(s_gate, m + 1)
                act.wait_ge(s_conv, m)
                nc.scalar.activation(g(tmp), grid(0), ACT.Copy, scale=cw[:, c, 0:1]).then_inc(s_tap, 1)
                act.wait_ge(s_conv, m + 1)
                nc.scalar.activation(sq[:, c, 0:n], tmp[:, 0:n], ACT.Square).then_inc(s_sq, 1)
                nc.scalar.activation(out, tmp[:, 0:n], ACT.Copy, scale=gcv[:, c:c + 1]).then_inc(s_cat, 1)

            def save(i, cols, k):
                act.wait_ge(s_ss, i + 1)
                nc.scalar.activation(cols, psQ[:, 0:k], ACT.Copy).then_inc(s_sse, 1)

            with act.Fori(0, STEPS) as i:
                round_x(i, xh[:].rearrange("p k (a t) -> p a k t", a=4), xr[:])
                act.wait_ge(s_st, 16 * (i + 1))
                act.wait_ge(s_ss, i)
                for c in range(CC):
                    chunk(CC * i + c, c, N, lambda t: t[:], lambda k: gated[:, c, k:k + N],
                          cat[:, :, c, :])
                save(i, ssc[:, bass.ds(4 * i, 4)], 4)
            round_x(STEPS, xh[:, :, 0:P], xr[:, 0])
            act.wait_ge(s_st, 16 * (STEPS + 1))
            act.wait_ge(s_ss, STEPS)
            for c in range(CC):
                chunk(CC * STEPS + c, c, P, lambda t: t[:, 0:NSAMP].rearrange("p (b t) -> p b t", b=DEC_B),
                      lambda k: gs[:, c, :, k:k + DEC_S], cat[:, 0, c, :])
            save(STEPS, ssc[:, PT_TILES:TILES], 1)

        @block.vector
        def _(dve):
            nc.vector.memset(gated[:], 0.0)
            nc.vector.memset(cat[:], 0.0)
            nc.vector.memset(tmp[:], 0.0)
            nc.vector.memset(ones[:], 1.0)
            dve.drain().then_inc(s_zero, 1)
            w_dve(dve)
            dve.wait_ge(s_const, 48)

            def split_x(i, dst, src, hi):
                dve.wait_ge(s_xh, i + 1)
                nc.vector.tensor_tensor(dst, src, hi.bitcast(F32), ALU.subtract).then_inc(s_xl, 1)

            def chunk(m, c, view, n, mid, grid):
                dve.wait_ge(s_u, m + 1)
                dve.wait_ge(s_proj, 3 * m + 2)
                nc.vector.tensor_tensor(mid, view(psG[:, c % 2, 1, :]), view(us), ALU.mult).then_inc(s_gate, 1)
                dve.wait_ge(s_tap, m + 1)
                nc.vector.scalar_tensor_tensor(view(tmp), grid(1), cw[:, c, 1:2], view(tmp), ALU.mult, ALU.add)
                dve.drain()
                nc.vector.scalar_tensor_tensor(view(tmp), grid(2), cw[:, c, 2:3], view(tmp), ALU.mult, ALU.add)
                dve.drain()
                dve.wait_ge(s_proj, 3 * m + 3)
                nc.vector.tensor_tensor(view(tmp), view(tmp), view(psG[:, c % 2, 2, :]), ALU.mult).then_inc(s_conv, 1)

            with dve.Fori(0, STEPS) as i:
                split_x(i, xl[:].rearrange("p k (a t) -> p a k t", a=4), xr[:],
                        xh[:].rearrange("p k (a t) -> p a k t", a=4))
                for c in range(CC):
                    chunk(CC * i + c, c, lambda t: t[:, 0:N], N, gated[:, c, 2:N + 2],
                          lambda k: gated[:, c, k:k + N])
                dve.drain()
                nc.vector.tensor_copy(gated[:, :, 0:2], gated[:, :, N:N + 2])
            dve.drain()
            split_x(STEPS, xl[:, :, 0:P], xr[:, 0], xh[:, :, 0:P])
            samp = lambda t: t[:, 0:NSAMP].rearrange("p (b t) -> p b t", b=DEC_B)
            for c in range(CC):
                chunk(CC * STEPS + c, c, samp, P, gs[:, c, :, 2:DEC_S + 2],
                      lambda k: gs[:, c, :, k:k + DEC_S])

        @block.tensor
        def _(pe):
            pe.wait_ge(s_w, n_w)
            pe.wait_ge(s_zero, 1)

            def step(i, n):
                pe.wait_ge(s_xl, i + 1)
                for c in range(CC):
                    m = CC * i + c
                    if c >= 2:
                        pe.wait_ge(s_conv, m - 1)
                    else:
                        pe.wait_ge(s_conv, CC * i)
                    for j, col in enumerate((0, 2, 1)):
                        for kc in range(KC):
                            for q, (a, b) in enumerate(((wh, xh), (wl, xh), (wh, xl))):
                                last = nc.tensor.matmul(psG[:, c % 2, j, 0:n],
                                                        a[:, kc, col * CH + c * P:col * CH + (c + 1) * P],
                                                        b[:, kc, 0:n], start=(kc == 0 and q == 0),
                                                        stop=(kc == KC - 1 and q == 2))
                        last.then_inc(s_proj, 1)

            def sums(i, tiles):
                pe.wait_ge(s_sq, CC * (i + 1))
                pe.wait_ge(s_sse, i)
                for a in range(tiles):
                    for c in range(CC):
                        last = nc.tensor.matmul(psQ[:, a:a + 1], sq[:, c, a * P:(a + 1) * P], ones[:, 0:1],
                                                start=(c == 0), stop=(c == CC - 1))
                last.then_inc(s_ss, 1)

            with pe.Fori(0, STEPS) as i:
                step(i, N)
                sums(i, 4)
            step(STEPS, P)
            sums(STEPS, 1)


def stage_dense(nc, io, ov):
    with ExitStack() as ctx:
        ph = Phase(nc, ctx, "de")
        sb, ps, sem = ph.sb, ph.ps, ph.sem
        woh, wol = sb("woh", [P, KC, D], F32R), sb("wol", [P, KC, D], F32R)
        guh, gul = sb("guh", [P, KC, 2 * FF], F32R), sb("gul", [P, KC, 2 * FF], F32R)
        dnh, dnl = sb("dnh", [P, FC, D], F32R), sb("dnl", [P, FC, D], F32R)
        rwh, rwl = sb("rwh", [P, KC, NE], F32R), sb("rwl", [P, KC, NE], F32R)
        cr = sb("cr", [P, KC, P])
        ch, cl = sb("ch", [P, KC, P], F32R), sb("cl", [P, KC, P], F32R)
        hTh, hTl = sb("hTh", [P, KC, P], F32R), sb("hTl", [P, KC, P], F32R)
        xr, t = sb("xr", [P, D]), sb("t", [P, D])
        raw = sb("raw", [P, 2, 2 * D])
        h = sb("h", [P, 2, D])
        acc = sb("acc", [P, D])
        lg, lb = sb("lg", [P, D]), sb("lb", [P, D])
        ident, ones = sb("ident", [P, P]), sb("ones", [P, 2])
        hid, sg = sb("hid", [P, FF]), sb("sg", [P, FF])
        hdh, hdl = sb("hdh", [P, FC, P], F32R), sb("hdl", [P, FC, P], F32R)
        ssa, ssc = sb("ssa", [P, TILES + 1]), sb("ssc", [P, TILES])
        ra, rc = sb("ra", [P, TILES]), sb("rc", [P, TILES])
        st, mv, rs = sb("st", [P, 2, 6]), sb("mv", [P, 2]), sb("rs", [P, 4])
        vd, drop = sb("vd", [P, TILES]), sb("drop", [P, TILES, TOPK])
        tokid, base = sb("tokid", [P, TILES], I32), sb("base", [P, NE])
        rbias, sc, sel = sb("rbias", [P, NE]), sb("sc", [P, NE]), sb("sel", [P, NE])
        gm, gp, gr = sb("gm", [P, NG, 8]), sb("gp", [P, NG + TOPG]), sb("gr", [P, NG + TOPG])
        pen, g8, s8, d8 = sb("pen", [P, NG]), sb("g8", [P, 8]), sb("s8", [P, 8]), sb("d8", [P, 8])
        sp_, sr = sb("selp", [P, NE + 2]), sb("sr", [P, NE + 2])
        mk, gt, dd, junk = sb("mk", [P, NE]), sb("gt", [P, NE]), sb("dd", [P, NE]), sb("junk", [P, TOPK, NE])
        gsum, g6 = sb("gsum", [P, 2]), sb("g6", [P, TOPK])
        mkb, macc = sb("mkb", [P, NE], BF16), sb("macc", [P, NE], BF16)
        trif, trib, oneb = sb("trif", [P, P]), sb("trib", [P, P], BF16), sb("oneb", [P, P], BF16)
        dest, pay = sb("dest", [P, TOPK], I32), sb("pay", [P, TOPK, 2], I32)
        thr, nidx, ecol = sb("thr", [NE, 8]), sb("nidx", [NE, OVMAX]), sb("ecol", [NE, 3])
        oc = sb("oc", [NE, 4]); oi, oq, oj = sb("oi", [NE, OVMAX]), sb("oq", [NE, OVMAX]), sb("oj", [NE, 8])

        psA, psC = ps("psA", [P, D]), ps("psC", [P, D])
        psT = ps("psT", [P, D])
        psU, psR = ps("psU", [P, 2 * FF]), ps("psR", [P, 512])

        names = ("const", "passed", "sums", "zero", "cat_loaded", "x_loaded", "cat_hi", "cat_lo", "wo", "wo_act", "wo_read", "var", "std",
                 "rstd", "norm", "h", "h_stored", "hT", "hT_hi", "hT_lo", "logit", "score", "gu", "sig", "hid",
                 "hidT", "hid_hi", "hid_lo", "down", "acc", "acc_stored", "mask", "rank", "rank_read", "pay", "scat",
                 "init", "gscaled", "gscale", "ovA", "ovB", "ovC", "ovD", "ovE", "ovF")
        S = {n: sem(n) for n in names}
        pieces = [(io["w_out"][:, k:k + 2], woh[:, k:k + 2, :], wol[:, k:k + 2, :]) for k in range(0, KC, 2)]
        for j, w in enumerate(("ws_gate", "ws_up")):
            pieces.append((io[w], guh[:, :, j * FF:(j + 1) * FF], gul[:, :, j * FF:(j + 1) * FF]))
        pieces += [(io["router_w"], rwh[:], rwl[:]), (io["ws_down"], dnh[:], dnl[:])]
        w_sp, w_act, w_dve, s_w, n_w = split_weights(nc, ph, pieces, raw)
        consts = [(ident[:], io["ident"]), (lg[:], io["ln1_g"].partition_broadcast(P)),
                  (lb[:], io["ln1_b"].partition_broadcast(P)), (ssa[:], io["ssA"]), (ssc[:], io["ssC"]),
                  (vd[:], io["valid"]), (drop[:], io["drop"]), (tokid[:], io["tokid"]), (base[:], io["base"]),
                  (rbias[:], io["router_bias"].partition_broadcast(P)), (trif[:], io["tri"]),
                  (thr[:], io["thr"]), (nidx[:], io["nidx"]), (ecol[:], io["ecol"])]
        CONST = 16 * len(consts)
        LAST = TILES - 1

        def steps(eng, step):
            step(0, 0, True, True, True)
            with eng.Fori(0, (LAST - 2) // 2) as j:
                step(2 * j + 1, 1, False, True, True)
                step(2 * j + 2, 0, False, True, True)
            step(LAST - 1, 1, False, False, True)
            step(LAST, 0, False, False, False)

        block = ctx.enter_context(nc.Block())

        @block.sync
        def _(sp):
            for dst, src in consts:
                sp.dma_start(dst, src).then_inc(S["const"], 16)
            sp.dma_start(io["table"][0:DROP_SLOT], io["table0"]).then_inc(S["init"], 16)

            def load_cat(i):
                sp.wait_ge(S["cat_lo"], i)
                sp.dma_start(cr[:, 0:GQ], io["catA"][bass.ds(i + 1, 1)].rearrange("o p k t -> (o p) k t")).then_inc(S["cat_loaded"], 16)
                sp.dma_start(cr[:, GQ:KC], io["catC"][bass.ds(i + 4, 1)].rearrange("o p k t -> (o p) k t")).then_inc(S["cat_loaded"], 16)

            def load_x(i):
                sp.wait_ge(S["norm"], i)
                sp.dma_start(xr[:], io["x_rows"][bass.ds(i * P, P)]).then_inc(S["x_loaded"], 16)

            load_cat(0)
            load_x(0)
            w_sp(sp)
            load_cat(1)
            sp.wait_ge(S["zero"], 1)
            sp.dma_start(io["h_d"][TPAD:ROWS], acc[:]).then_inc(S["init"], 16)
            sp.dma_start(io["acc_d"][TPAD:ROWS], acc[:]).then_inc(S["init"], 16)

            def step(i, k, first, pre, front):
                if front:
                    load_x(i + 1)
                if pre:
                    load_cat(i + 2)
                if not first:
                    sp.wait_ge(S["acc"], i)
                    sp.dma_start(io["acc_d"][bass.ds((i - 1) * P, P)], acc[:]).then_inc(S["acc_stored"], 16)

            steps(sp, step)
            sp.wait_ge(S["acc"], TILES)
            sp.dma_start(io["acc_d"][bass.ds(LAST * P, P)], acc[:]).then_inc(S["acc_stored"], 16)
            sp.wait_ge(S["acc_stored"], 16 * TILES)
            sp.wait_ge(S["ovF"], 1)

        @block.gpsimd
        def _(pool):
            pool.wait_ge(S["const"], CONST)

            def gain(i, k):
                pool.wait_ge(S["norm"], i + 1)
                nc.gpsimd.tensor_tensor(h[:, k, :], h[:, k, :], lg[:], ALU.mult).then_inc(S["gscaled"], 1)
                pool.wait_ge(S["gscaled"], i + 1)
                nc.gpsimd.tensor_tensor(h[:, k, :], h[:, k, :], lb[:], ALU.add).then_inc(S["h"], 1)
                hold(pool, S["h"], i + 1, S["passed"])
                hold(pool, S["h_stored"], 16 * i, S["passed"])
                pool.dma_start(io["h_d"][bass.ds(i * P, P)], h[:, k, :]).then_inc(S["h_stored"], 16)

            def step(i, k, first, pre, front):
                if front:
                    gain(i + 1, 1 - k)
                if not first:
                    scatter(i - 1)

            def scatter(i):
                hold(pool, S["pay"], i + 1, S["passed"])
                for j in range(TOPK):
                    nc.gpsimd.indirect_dma_start(
                        out=io["table"], out_offset=bass.IndirectOffsetOnAxis(ap=dest[:, j:j + 1].bitcast(U32), axis=0),
                        in_=pay[:, j, :], in_offset=None).then_inc(S["scat"], 16)

            gain(0, 0)
            pool.wait_ge(S["init"], 48)
            steps(pool, step)
            scatter(LAST)
            pool.wait_ge(S["scat"], 16 * TOPK * TILES)
            pool.wait_ge(S["h_stored"], 16 * TILES)

        @block.scalar
        def _(act):
            def round_cat(i):
                act.wait_ge(S["cat_loaded"], 32 * (i + 1))
                act.wait_ge(S["wo"], i)
                nc.scalar.activation(ch[:], cr[:], ACT.Copy).then_inc(S["cat_hi"], 1)

            def scale_attention(i):
                act.wait_ge(S["wo"], i + 1)
                nc.scalar.activation(t[:], psA[:], ACT.Copy, scale=ra[:, bass.ds(i, 1)]).then_inc(S["wo_act"], 1)

            def norm(i, k, fresh):
                act.wait_ge(S["var"], i + 1)
                nc.scalar.activation(rs[:, 1:2], rs[:, 0:1], ACT.Sqrt).then_inc(S["std"], 1)
                act.wait_ge(S["rstd"], i + 1)
                if not fresh:
                    act.wait_ge(S["hT"], i - 1)
                    act.wait_ge(S["acc"], i - 1)
                    act.wait_ge(S["h_stored"], 16 * (i - 1))
                nc.scalar.activation(h[:, k, :], t[:], ACT.Identity, scale=rs[:, 2:3], bias=rs[:, 3:4]).then_inc(S["norm"], 1)

            round_cat(0)
            w_act(act)
            act.wait_ge(S["sums"], 1)
            nc.scalar.activation(ra[:], ra[:], ACT.Sqrt)
            nc.scalar.activation(rc[:], rc[:], ACT.Sqrt).then_inc(S["sums"], 1)
            act.wait_ge(S["sums"], 3)
            scale_attention(0)
            round_cat(1)
            norm(0, 0, True)

            def hidden(i):
                act.wait_ge(S["hidT"], i + 1)
                act.wait_ge(S["down"], i)
                nc.scalar.activation(hdh[:].rearrange("p f t -> p (f t)"), psR[:, 128:384], ACT.Copy).then_inc(S["hid_hi"], 1)

            def step(i, k, first, pre, front):
                act.wait_ge(S["hT"], i + 1)
                act.wait_ge(S["gu"], i)
                nc.scalar.activation(hTh[:].rearrange("p k t -> p (k t)"), psT[:], ACT.Copy).then_inc(S["hT_hi"], 1)
                if not first:
                    hidden(i - 1)
                if front:
                    scale_attention(i + 1)
                if pre:
                    round_cat(i + 2)
                if front:
                    norm(i + 1, 1 - k, first)
                act.wait_ge(S["logit"], i + 1)
                act.wait_ge(S["gscale"], i)
                nc.scalar.activation(sc[:], psR[:, 0:NE], ACT.Sigmoid).then_inc(S["score"], 1)
                act.wait_ge(S["gu"], i + 1)
                act.wait_ge(S["hid"], i)
                nc.scalar.activation(sg[:], psU[:, 0:FF], ACT.Sigmoid).then_inc(S["sig"], 1)

            steps(act, step)
            hidden(LAST)

        @block.vector
        def _(dve):
            V = nc.vector

            def split_cat(i):
                dve.wait_ge(S["cat_hi"], i + 1)
                V.tensor_tensor(cl[:], cr[:], ch[:].bitcast(F32), ALU.subtract).then_inc(S["cat_lo"], 1)

            def residual(i):
                dve.wait_ge(S["wo_act"], i + 1)
                V.scalar_tensor_tensor(t[:], psC[:], rc[:, bass.ds(i, 1)], t[:], ALU.mult, ALU.add).then_inc(S["wo_read"], 1)
                dve.wait_ge(S["wo_read"], i + 1)
                dve.wait_ge(S["x_loaded"], 16 * (i + 1))
                V.scalar_tensor_tensor(t[:], xr[:], ALPHA, t[:], ALU.mult, ALU.add)
                dve.drain()
                for a in range(2):
                    V.bn_stats(st[:, a, :], t[:, a * 512:(a + 1) * 512])
                dve.drain()
                V.bn_aggr(mv[:], st[:])
                dve.drain()
                V.tensor_scalar(rs[:, 0:1], mv[:, 1:2], LN_EPS, None, ALU.add).then_inc(S["var"], 1)
                dve.wait_ge(S["std"], i + 1)
                V.reciprocal(rs[:, 2:3], rs[:, 1:2])
                dve.drain()
                V.scalar_tensor_tensor(rs[:, 3:4], mv[:, 0:1], -1.0, rs[:, 2:3], ALU.mult, ALU.mult).then_inc(S["rstd"], 1)

            def hidden(i):
                dve.wait_ge(S["hid_hi"], i + 1)
                V.tensor_tensor(hdl[:].rearrange("p f t -> p (f t)"), psR[:, 128:384],
                                hdh[:].bitcast(F32).rearrange("p f t -> p (f t)"), ALU.subtract).then_inc(S["hid_lo"], 1)

            def accumulate(i, k):
                dve.wait_ge(S["down"], i + 1)
                dve.wait_ge(S["acc_stored"], 16 * i)
                V.scalar_tensor_tensor(acc[:], h[:, k, :], ALPHA, psT[:], ALU.mult, ALU.add).then_inc(S["acc"], 1)

            def pick(i):
                dve.wait_ge(S["score"], i + 1)
                V.tensor_tensor(sel[:], sc[:], rbias[:], ALU.add)
                dve.drain()
                for g in range(NG):
                    V.max(gm[:, g, :], sel[:, g * EPG:(g + 1) * EPG])
                dve.drain()
                V.tensor_tensor(gp[:, 0:NG], gm[:, :, 0], gm[:, :, 1], ALU.add)
                dve.drain()
                V.max(g8[:], gp[:])
                dve.drain()
                V.match_replace(gr[:], g8[:], gp[:], -BIG)
                dve.drain()
                V.tensor_scalar(pen[:], gr[:, 0:NG], -BIG, NEG, ALU.not_equal, ALU.mult)
                dve.drain()
                V.tensor_tensor(sp_[:, 0:NE].rearrange("p (g e) -> p g e", g=NG), sel[:].rearrange("p (g e) -> p g e", g=NG),
                                pen[:].unsqueeze(2).to_broadcast([P, NG, EPG]), ALU.add)
                dve.drain()
                V.max(s8[:], sp_[:])
                dve.drain()
                V.match_replace(sr[:], s8[:], sp_[:], -BIG)
                dve.drain()
                V.tensor_scalar(mk[:], sr[:, 0:NE], -BIG, None, ALU.is_equal)
                V.tensor_scalar(mkb[:], sr[:, 0:NE], -BIG, vd[:, bass.ds(i, 1)], ALU.is_equal, ALU.mult).then_inc(S["mask"], 1)
                dve.drain()
                V.scalar_tensor_tensor(gt[:], sc[:], 1.0, mk[:], ALU.mult, ALU.mult, accum_out=gsum[:, 0:1])
                dve.drain()
                V.reciprocal(gsum[:, 1:2], gsum[:, 0:1])
                dve.drain()
                V.tensor_scalar(gt[:], gt[:], gsum[:, 1:2], 2.5, ALU.mult, ALU.mult).then_inc(S["gscale"], 1)

            def place(i):
                dve.wait_ge(S["gscale"], i + 1)
                dve.wait_ge(S["rank"], i + 1)
                V.tensor_tensor(dd[:], psR[:, NE:2 * NE], base[:], ALU.add).then_inc(S["rank_read"], 1)
                V.tensor_tensor(macc[:], macc[:], mkb[:], ALU.add)
                dve.drain()
                V.tensor_tensor(dd[:], dd[:], mkb[:], ALU.mult)
                dve.drain()
                V.max(d8[:], dd[:])
                dve.drain()
                for j in range(TOPK):
                    V.scalar_tensor_tensor(junk[:, j], dd[:], d8[:, j:j + 1], gt[:], ALU.is_equal, ALU.mult,
                                           accum_out=g6[:, j:j + 1])
                dve.wait_ge(S["scat"], 16 * TOPK * i)
                V.scalar_tensor_tensor(dest[:], d8[:, 0:TOPK], -1.0, drop[:, bass.ds(i, 1), :].rearrange("p o j -> p (o j)"),
                                       ALU.add, ALU.add)
                V.tensor_copy(pay[:, :, 0], tokid[:, bass.ds(i, 1)].to_broadcast([P, TOPK]))
                dve.drain()
                V.tensor_copy(pay[:, :, 1].bitcast(F32), g6[:])
                dve.drain().then_inc(S["pay"], 1)

            V.memset(acc[:], 0.0).then_inc(S["zero"], 1)
            V.memset(ones[:], 1.0)
            V.memset(oneb[:], 1.0)
            V.memset(macc[:], 0.0)
            V.memset(gp[:], BIG)
            V.memset(sp_[:], BIG)
            dve.wait_ge(S["const"], CONST)
            V.tensor_copy(trib[:], trif[:])
            dve.drain().then_inc(S["zero"], 1)
            split_cat(0)
            w_dve(dve)
            V.tensor_scalar(ra[:], ssa[:, 1:TILES + 1], 1.0 / AW, RMS_EPS, ALU.mult, ALU.add)
            V.tensor_scalar(rc[:], ssc[:], 1.0 / CH, RMS_EPS, ALU.mult, ALU.add).then_inc(S["sums"], 1)
            dve.wait_ge(S["sums"], 2)
            V.reciprocal(ra[:], ra[:])
            V.reciprocal(rc[:], rc[:]).then_inc(S["sums"], 1)
            dve.wait_ge(S["sums"], 3)
            residual(0)
            split_cat(1)
            dve.wait_ge(S["init"], 48)

            def step(i, k, first, pre, front):
                dve.wait_ge(S["hT_hi"], i + 1)
                V.tensor_tensor(hTl[:].rearrange("p k t -> p (k t)"), psT[:], hTh[:].bitcast(F32).rearrange("p k t -> p (k t)"),
                                ALU.subtract).then_inc(S["hT_lo"], 1)
                if not first:
                    hidden(i - 1)
                    place(i - 1)
                if front:
                    residual(i + 1)
                if not first:
                    accumulate(i - 1, 1 - k)
                if pre:
                    split_cat(i + 2)
                dve.wait_ge(S["sig"], i + 1)
                V.tensor_tensor(hid[:], psU[:, 0:FF], sg[:], ALU.mult)
                dve.drain()
                V.tensor_tensor(hid[:], hid[:], psU[:, FF:2 * FF], ALU.mult).then_inc(S["hid"], 1)
                pick(i)

            steps(dve, step)
            hidden(LAST)
            place(LAST)
            accumulate(LAST, 0)

            dve.wait_ge(S["ovA"], 1)
            V.tensor_copy(oc[:, 0:1], psR[0:NE, 0:1])
            dve.drain()
            V.tensor_scalar(oj[:], thr[:], oc[:, 0:1], None, ALU.is_lt)
            dve.drain()
            V.tensor_reduce(oc[:, 1:2], oj[:], AX_X, ALU.add)
            dve.drain().then_inc(S["ovB"], 1)
            dve.wait_ge(S["ovC"], 1)
            V.tensor_copy(oc[:, 2:3], psR[0:NE, 1:2])
            dve.drain()
            V.tensor_tensor(oc[:, 3:4], oc[:, 2:3], oc[:, 1:2], ALU.add)
            dve.drain()
            V.tensor_scalar(oi[:], nidx[:], oc[:, 2:3], None, ALU.is_ge)
            dve.drain()
            V.scalar_tensor_tensor(oi[:], nidx[:], oc[:, 3:4], oi[:], ALU.is_lt, ALU.mult)
            dve.drain()
            V.scalar_tensor_tensor(oq[:], nidx[:], oc[:, 2:3], oi[:], ALU.subtract, ALU.mult)
            dve.drain().then_inc(S["ovD"], 1)
            dve.wait_ge(S["ovE"], 1)
            V.tensor_copy(ov[:, 0:OVMAX], psR[0:1, 64:64 + OVMAX])
            V.tensor_scalar(ov[:, OVMAX:2 * OVMAX], psR[0:1, 128:128 + OVMAX], float(TRASH_SLOT), None, ALU.add)
            V.tensor_scalar(oj[0:1, 0:1], psR[0:1, 192:193], 1.0, None, ALU.mult)
            dve.drain()
            V.tensor_scalar(oq[0:1, 0:OVP], nidx[0:1, 0:OVMAX:2], oj[0:1, 0:1], None, ALU.is_lt)
            dve.drain()
            V.tensor_reduce(oj[0:1, 1:2], oq[0:1, 0:OVP], AX_X, ALU.add)
            dve.drain()
            V.tensor_copy(ov[:, 2 * OVMAX:2 * OVMAX + 1], oj[0:1, 1:2])
            dve.drain().then_inc(S["ovF"], 1)

        @block.tensor
        def _(pe):
            pe.wait_ge(s_w, n_w)
            pe.wait_ge(S["zero"], 2)

            def three(out, lh, ll, rh, rl, start, stop):
                nc.tensor.matmul(out, lh, rh, start=start, stop=False)
                nc.tensor.matmul(out, lh, rl, start=False, stop=False)
                return nc.tensor.matmul(out, ll, rh, start=False, stop=stop)

            def project(i, part):
                if part == 0:
                    pe.wait_ge(S["cat_lo"], i + 1)
                    pe.wait_ge(S["wo_read"], i)
                c0, c1, out = ((0, GQ, psA), (GQ, KC, psC))[part]
                for hf in range(2):
                    cols = slice(hf * 512, (hf + 1) * 512)
                    for c in range(c0, c1):
                        last = three(out[:, cols], ch[:, c, :], cl[:, c, :], woh[:, c, cols], wol[:, c, cols],
                                     c == c0, c == c1 - 1)
                if part == 1:
                    last.then_inc(S["wo"], 1)

            def rank(i):
                pe.wait_ge(S["mask"], i + 1)
                pe.wait_ge(S["pay"], i)
                pe.wait_ge(S["hid_lo"], i + 1)
                nc.tensor.matmul(psR[:, NE:2 * NE], trib[:], mkb[:], start=True, stop=False)
                nc.tensor.matmul(psR[:, NE:2 * NE], oneb[:], macc[:], start=False, stop=True).then_inc(S["rank"], 1)

            def hidden_T(i):
                pe.wait_ge(S["hid"], i + 1)
                pe.wait_ge(S["score"], i + 1)
                pe.wait_ge(S["hid_lo"], i)
                for f in range(FC):
                    last = nc.tensor.transpose(psR[:, 128 + f * P:128 + (f + 1) * P], hid[:, f * P:(f + 1) * P], ident[:])
                last.then_inc(S["hidT"], 1)

            def down(i):
                pe.wait_ge(S["hid_lo"], i + 1)
                for hf in range(2):
                    cols = slice(hf * 512, (hf + 1) * 512)
                    for f in range(FC):
                        last = three(psT[:, cols], hdh[:, f, :], hdl[:, f, :], dnh[:, f, cols], dnl[:, f, cols],
                                     f == 0, f == FC - 1)
                last.then_inc(S["down"], 1)

            project(0, 0)
            project(0, 1)

            def step(i, k, first, pre, front):
                pe.wait_ge(S["h"], i + 1)
                if not first:
                    pe.wait_ge(S["acc"], i - 1)
                for kc in range(KC):
                    last = nc.tensor.transpose(psT[:, kc * P:(kc + 1) * P], h[:, k, kc * P:(kc + 1) * P], ident[:])
                last.then_inc(S["hT"], 1)
                if not first:
                    hidden_T(i - 1)
                if front:
                    project(i + 1, 0)
                if not first:
                    rank(i - 1)
                if front:
                    project(i + 1, 1)
                pe.wait_ge(S["hT_lo"], i + 1)
                if not first:
                    down(i - 1)
                pe.wait_ge(S["rank_read"], i)
                pe.wait_ge(S["hid"], i)
                for kc in range(KC):
                    last = three(psR[:, 0:NE], hTh[:, kc, :], hTl[:, kc, :], rwh[:, kc, :], rwl[:, kc, :], kc == 0, kc == KC - 1)
                last.then_inc(S["logit"], 1)
                for kc in range(KC):
                    last = three(psU[:], hTh[:, kc, :], hTl[:, kc, :], guh[:, kc, :], gul[:, kc, :], kc == 0, kc == KC - 1)
                last.then_inc(S["gu"], 1)

            steps(pe, step)
            hidden_T(LAST)
            rank(LAST)
            down(LAST)
            pe.wait_ge(S["pay"], TILES)
            pe.wait_ge(S["hid_lo"], TILES)
            nc.tensor.matmul(psR[0:NE, 0:1], macc[:], oneb[:, 0:1], start=True, stop=True).then_inc(S["ovA"], 1)
            pe.wait_ge(S["ovB"], 1)
            nc.tensor.matmul(psR[0:NE, 1:2], trif[0:NE, 0:NE], oc[:, 1:2], start=True, stop=True).then_inc(S["ovC"], 1)
            pe.wait_ge(S["ovD"], 1)
            nc.tensor.matmul(psR[0:1, 64:64 + OVMAX], ecol[:, 0:1], oi[:], start=True, stop=True)
            nc.tensor.matmul(psR[0:1, 128:128 + OVMAX], ecol[:, 1:2], oi[:], start=True, stop=False)
            nc.tensor.matmul(psR[0:1, 128:128 + OVMAX], ecol[:, 2:3], oq[:], start=False, stop=True)
            nc.tensor.matmul(psR[0:1, 192:193], oc[:, 1:2], ones[0:NE, 0:1], start=True, stop=True).then_inc(S["ovE"], 1)


def stage_experts(nc, io, ov):
    PAIRS = NE // 2
    with ExitStack() as ctx:
        ph = Phase(nc, ctx, "ex")
        sb, ps, sem = ph.sb, ph.ps, ph.sem
        raw = sb("raw", [P, 2, 3, 2048])
        guh, gul = sb("guh", [P, 2, KC, 2 * FF], F32R), sb("gul", [P, 2, KC, 2 * FF], F32R)
        dnh, dnl = sb("dnh", [P, 2, FC, D], F32R), sb("dnl", [P, 2, FC, D], F32R)
        xg = sb("xg", [P, 4, D])
        xh, xl = sb("xh", [P, 2, KC, P], F32R), sb("xl", [P, 2, KC, P], F32R)
        sg, hid = sb("sg", [P, FF]), sb("hid", [P, 2, FF])
        hdh, hdl = sb("hdh", [P, FC, P], F32R), sb("hdl", [P, FC, P], F32R)
        y = sb("y", [P, 4, D])
        ent = sb("ent", [P, 4, 2], I32)
        use = sb("use", [P, 4, 2], I32)
        ident = sb("ident", [P, P])
        psX, psU = ps("psX", [P, D]), ps("psU", [P, 2, 2 * FF])
        psH, psY = ps("psH", [P, FC * P]), ps("psY", [P, D])

        s_const, s_passed, s_sp_passed = sem("const"), sem("passed"), sem("sp_passed")
        s_w = [[sem(f"{n}_loaded{b}") for n in ("gate", "up", "down")] for b in range(2)]
        s_round, s_split = sem("rounded"), sem("split")
        s_ent = [sem(f"entries{b}") for b in range(2)]
        s_row = [sem(f"rows{k}") for k in range(4)]
        s_use, s_add, s_y = sem("entries_kept"), sem("added"), sem("y")
        s_xT, s_xh, s_xl = sem("xT"), sem("xT_hi"), sem("xT_lo")
        s_gu, s_sig, s_hid = sem("gate_up"), sem("sig"), sem("hid")
        s_hT, s_hh, s_hl, s_dn = sem("hidT"), sem("hidT_hi"), sem("hidT_lo"), sem("down")

        PIECES = [(b, kind, part) for b in range(2) for kind in (0, 1, 2) for part in range(2)]
        STEP_PIECES = (range(0, 4), range(4, 7), range(7, 10), range(10, 12))

        def piece(n):
            b, kind, part = PIECES[n]
            src = raw[:, b, kind, part * 1024:(part + 1) * 1024]
            if kind < 2:
                k0 = part * KC // 2
                at = (slice(None), b, slice(k0, k0 + KC // 2), slice(kind * FF, (kind + 1) * FF))
                return src.rearrange("p (k f) -> p k f", f=FF), guh[at], gul[at]
            return src, dnh[:, b, part, :], dnl[:, b, part, :]

        def pairs(eng, pair):
            pair(0, True, None)
            with eng.Fori(1, PAIRS) as p:
                pair(p, False, None)
            more = eng.value_load(ov[0:1, 2 * OVMAX:2 * OVMAX + 1], min_val=0, max_val=OVP)
            with eng.Fori(0, OVP) as j:
                with eng.If(more > j):
                    pair(PAIRS + j, False, j)
            return PAIRS + more

        block = ctx.enter_context(nc.Block())

        @block.sync
        def _(sp):
            sp.dma_start(ident[:], io["ident"]).then_inc(s_const, 16)

            def pair(p, first, j):
                for b in range(2):
                    if j is None:
                        e = 2 * p + b
                        slot = e * SLOTS
                    else:
                        e = sp.value_load(ov[0:1, bass.ds(2 * j + b, 1)], min_val=0, max_val=NE - 1)
                        slot = sp.value_load(ov[0:1, bass.ds(2 * j + b + OVMAX, 1)], min_val=0, max_val=TRASH_SLOT)
                    if not first:
                        hold(sp, s_use, 4 * p + 2 * b - 2, s_sp_passed)
                        hold(sp, s_row[2 * b], 16 * p, s_sp_passed)
                        hold(sp, s_row[2 * b + 1], 16 * p, s_sp_passed)
                    sp.dma_start(ent[:, 2 * b:2 * b + 2, :],
                                 io["table"][bass.ds(slot, BLK)].rearrange("(t p) c -> p t c", p=P)).then_inc(s_ent[b], 16)
                    if not first:
                        hold(sp, s_split, 12 * p + 6 * b - 6, s_sp_passed)
                    for kind, name in enumerate(("w_gate", "w_up", "w_down")):
                        w = io[name][bass.ds(e, 1)].rearrange("o (k p) n -> (o p) k n", p=P)
                        sp.dma_start(raw[:, b, kind].rearrange("p (k n) -> p k n", n=w.shape[2]), w).then_inc(s_w[b][kind], 16)

            pairs(sp, pair)

        @block.gpsimd
        def _(pool):
            def add_rows(n, k, check):
                hold(pool, s_y, n + 1, s_passed)
                nc.gpsimd.indirect_dma_start(
                    out=io["acc_d"], out_offset=bass.IndirectOffsetOnAxis(ap=use[:, k, 0:1].bitcast(U32), axis=0),
                    in_=y[:, k, :], in_offset=None, compute_op=ALU.add).then_inc(s_add, 16)
                hold(pool, s_add, 16 * (n + 1), s_passed)

            def pair(p, first, j):
                for k in range(4):
                    n = 4 * p + k
                    if k % 2 == 0:
                        hold(pool, s_ent[k // 2], 16 * (p + 1), s_passed)
                    if not first:
                        hold(pool, s_xT, n - 3, s_passed)
                    nc.gpsimd.indirect_dma_start(
                        out=xg[:, k, :], out_offset=None, in_=io["h_d"],
                        in_offset=bass.IndirectOffsetOnAxis(ap=ent[:, k, 0:1].bitcast(U32), axis=0)).then_inc(s_row[k], 16)
                    if not first:
                        add_rows(n - 4, k, True)
                    nc.gpsimd.tensor_copy(use[:, k, :], ent[:, k, :]).then_inc(s_use, 1)
                    hold(pool, s_use, n + 1, s_passed)

            end = pairs(pool, pair)
            for k in range(4):
                add_rows(4 * end - 4 + k, k, True)

        def step_parts(first, k):
            return not (first and k < 1), not (first and k < 2)

        @block.scalar
        def _(act):
            A = nc.scalar

            def hidden(m):
                act.wait_ge(s_hT, m + 1)
                act.wait_ge(s_dn, m)
                A.activation(hdh[:].rearrange("p f t -> p (f t)"), psH[:], ACT.Copy).then_inc(s_hh, 1)

            def sigmoid(m, k):
                act.wait_ge(s_gu, m + 1)
                act.wait_ge(s_hid, m)
                A.activation(sg[:], psU[:, k % 2, 0:FF], ACT.Sigmoid).then_inc(s_sig, 1)

            def output(m, k, fresh):
                act.wait_ge(s_dn, m + 1)
                if not fresh:
                    act.wait_ge(s_add, 16 * (m - 2))
                A.activation(y[:, k % 4, :], psY[:], ACT.Copy).then_inc(s_y, 1)

            def split(p, first, k, part):
                todo = list(STEP_PIECES[k])
                half = len(todo) - 1
                for q in (todo[:half] if part == 0 else todo[half:]):
                    b, kind, half_ = PIECES[q]
                    act.wait_ge(s_w[b][kind], 16 * (p + 1))
                    if q in (0, 6) and not first:
                        act.wait_ge(s_gu, 4 * p - 2 + 2 * b)
                    if q in (4, 10) and not first:
                        act.wait_ge(s_dn, 4 * p - 2 + 2 * b)
                    src, hi, lo = piece(q)
                    A.activation(hi, src, ACT.Copy).then_inc(s_round, 1)

            def pair(p, first, j):
                for k in range(4):
                    n = 4 * p + k
                    has1, has2 = step_parts(first, k)
                    if has2:
                        hidden(n - 2)
                    split(p, first, k, 0)
                    if has1:
                        sigmoid(n - 1, k - 1)
                    act.wait_ge(s_xT, n + 1)
                    if not (first and k < 2):
                        act.wait_ge(s_gu, n - 1)
                    A.activation(xh[:, k % 2].rearrange("p k t -> p (k t)"), psX[:], ACT.Copy).then_inc(s_xh, 1)
                    split(p, first, k, 1)
                    if has2:
                        output(n - 2, k - 2, first)

            end = pairs(act, pair)
            n = 4 * end
            hidden(n - 2)
            sigmoid(n - 1, 3)
            output(n - 2, 2, False)
            hidden(n - 1)
            output(n - 1, 3, False)

        @block.vector
        def _(dve):
            V = nc.vector

            def hidden(m):
                dve.wait_ge(s_hh, m + 1)
                V.tensor_tensor(hdl[:].rearrange("p f t -> p (f t)"), psH[:],
                                hdh[:].bitcast(F32).rearrange("p f t -> p (f t)"), ALU.subtract).then_inc(s_hl, 1)

            def activate(m, k):
                dve.wait_ge(s_sig, m + 1)
                dve.wait_ge(s_use, m + 1)
                if not isinstance(m, int) or m >= 2:
                    dve.wait_ge(s_hT, m - 1)
                gate = use[:, k % 4, 1:2].bitcast(F32)
                V.scalar_tensor_tensor(hid[:, k % 2, :], psU[:, k % 2, 0:FF], gate, sg[:], ALU.mult, ALU.mult)
                dve.drain()
                V.tensor_tensor(hid[:, k % 2, :], hid[:, k % 2, :], psU[:, k % 2, FF:2 * FF], ALU.mult).then_inc(s_hid, 1)

            def split(p, first, k, part):
                todo = list(STEP_PIECES[k])
                half = len(todo) - 1
                for q in (todo[:half] if part == 0 else todo[half:]):
                    src, hi, lo = piece(q)
                    dve.wait_ge(s_round, 12 * p + q + 1)
                    V.tensor_tensor(lo, src, hi.bitcast(F32), ALU.subtract).then_inc(s_split, 1)

            def pair(p, first, j):
                for k in range(4):
                    n = 4 * p + k
                    has1, has2 = step_parts(first, k)
                    if has2:
                        hidden(n - 2)
                    split(p, first, k, 0)
                    if has1:
                        activate(n - 1, k - 1)
                    dve.wait_ge(s_xh, n + 1)
                    V.tensor_tensor(xl[:, k % 2].rearrange("p k t -> p (k t)"), psX[:],
                                    xh[:, k % 2].bitcast(F32).rearrange("p k t -> p (k t)"), ALU.subtract).then_inc(s_xl, 1)
                    split(p, first, k, 1)

            end = pairs(dve, pair)
            n = 4 * end
            hidden(n - 2)
            activate(n - 1, 3)
            hidden(n - 1)

        @block.tensor
        def _(pe):
            pe.wait_ge(s_const, 16)

            def three(out, lh, ll, rh, rl, start, stop):
                nc.tensor.matmul(out, lh, rh, start=start, stop=False)
                nc.tensor.matmul(out, lh, rl, start=False, stop=False)
                return nc.tensor.matmul(out, ll, rh, start=False, stop=stop)

            def hidden_T(m, k):
                pe.wait_ge(s_hid, m + 1)
                pe.wait_ge(s_hl, m)
                for f in range(FC):
                    last = nc.tensor.transpose(psH[:, f * P:(f + 1) * P], hid[:, k % 2, f * P:(f + 1) * P], ident[:])
                last.then_inc(s_hT, 1)

            def gate_up(m, k, b, pieces):
                pe.wait_ge(s_split, pieces)
                pe.wait_ge(s_xl, m + 1)
                if not isinstance(m, int) or m >= 1:
                    pe.wait_ge(s_hid, m - 1)
                for kc in range(KC):
                    last = three(psU[:, k % 2, :], xh[:, k % 2, kc, :], xl[:, k % 2, kc, :],
                                 guh[:, b, kc, :], gul[:, b, kc, :], kc == 0, kc == KC - 1)
                last.then_inc(s_gu, 1)

            def down(m, b, pieces):
                pe.wait_ge(s_hl, m + 1)
                pe.wait_ge(s_split, pieces)
                pe.wait_ge(s_y, m)
                for hf in range(2):
                    cols = slice(hf * 512, (hf + 1) * 512)
                    for f in range(FC):
                        last = three(psY[:, cols], hdh[:, f, :], hdl[:, f, :], dnh[:, b, f, cols], dnl[:, b, f, cols],
                                     f == 0, f == FC - 1)
                last.then_inc(s_dn, 1)

            GU_AT, DN_AT = (4, 4, 10, 10), (6, 6, 12, 12)

            def pair(p, first, j):
                for k in range(4):
                    n = 4 * p + k
                    has1, has2 = step_parts(first, k)
                    if has2:
                        hidden_T(n - 2, k - 2)
                    if has1:
                        q = (k - 1) % 4
                        gate_up(n - 1, k - 1, q // 2, 12 * p + GU_AT[q] - (12 if k < 1 else 0))
                    pe.wait_ge(s_row[k], 16 * (p + 1))
                    pe.wait_ge(s_xl, n)
                    for kc in range(KC):
                        last = nc.tensor.transpose(psX[:, kc * P:(kc + 1) * P], xg[:, k, kc * P:(kc + 1) * P], ident[:])
                    last.then_inc(s_xT, 1)
                    if has2:
                        q = (k - 2) % 4
                        down(n - 2, q // 2, 12 * p + DN_AT[q] - (12 if k < 2 else 0))

            end = pairs(pe, pair)
            n = 4 * end
            hidden_T(n - 2, 2)
            gate_up(n - 1, 3, 1, 12 * end - 2)
            down(n - 2, 1, 12 * end)
            hidden_T(n - 1, 3)
            down(n - 1, 1, 12 * end)


def stage_norm(nc, io):
    with ExitStack() as ctx:
        ph = Phase(nc, ctx, "ln")
        sb, sem = ph.sb, ph.sem
        B = 4
        t, z = sb("t", [P, B, D]), sb("z", [P, B, D])
        lg, lb = sb("lg", [P, D]), sb("lb", [P, D])
        st, mv, rs = sb("st", [P, B, 2, 6]), sb("mv", [P, B, 2]), sb("rs", [P, B, 4])
        s_const, s_passed, s_var, s_std, s_rstd, s_norm, s_gain, s_out = (sem(n) for n in ("const", "passed", "var", "std", "rstd", "norm", "gain", "out"))
        s_t, s_st = [sem(f"loaded{b}") for b in range(B)], [sem(f"stored{b}") for b in range(B)]
        block = ctx.enter_context(nc.Block())

        def tiles(eng, tile):
            for i in range(B):
                tile(i, i, 1)
            with eng.Fori(1, TILES // B) as j:
                for b in range(B):
                    tile(B * j + b, b, j + 1)
            tile(TILES - 1, 0, TILES // B + 1)

        @block.sync
        def _(sp):
            sp.dma_start(lg[:], io["ln2_g"].partition_broadcast(P)).then_inc(s_const, 16)
            sp.dma_start(lb[:], io["ln2_b"].partition_broadcast(P)).then_inc(s_const, 16)

            def tile(i, b, r):
                if not isinstance(r, int) or r > 1:
                    sp.wait_ge(s_norm, i - B + 1)
                sp.dma_start(t[:, b, :], io["acc_d"][bass.ds(i * P, P)]).then_inc(s_t[b], 16)

            tiles(sp, tile)

        @block.vector
        def _(dve):
            V = nc.vector
            dve.wait_ge(s_const, 32)

            def stats(i, b, r):
                dve.wait_ge(s_t[b], 16 * r)
                for a in range(2):
                    V.bn_stats(st[:, b, a, :], t[:, b, a * 512:(a + 1) * 512])
                dve.drain()
                V.bn_aggr(mv[:, b, :], st[:, b])
                dve.drain()
                V.tensor_scalar(rs[:, b, 0:1], mv[:, b, 1:2], LN_EPS, None, ALU.add).then_inc(s_var, 1)
                dve.wait_ge(s_std, i + 1)
                V.reciprocal(rs[:, b, 2:3], rs[:, b, 1:2])
                dve.drain()
                V.scalar_tensor_tensor(rs[:, b, 3:4], mv[:, b, 0:1], -1.0, rs[:, b, 2:3], ALU.mult, ALU.mult).then_inc(s_rstd, 1)
                dve.wait_ge(s_gain, i + 1)
                V.tensor_tensor(z[:, b, :], z[:, b, :], lb[:], ALU.add).then_inc(s_out, 1)

            tiles(dve, stats)

        @block.scalar
        def _(act):
            def tile(i, b, r):
                act.wait_ge(s_var, i + 1)
                nc.scalar.activation(rs[:, b, 1:2], rs[:, b, 0:1], ACT.Sqrt).then_inc(s_std, 1)
                act.wait_ge(s_rstd, i + 1)
                act.wait_ge(s_st[b], 16 * (r - 1))
                nc.scalar.activation(z[:, b, :], t[:, b, :], ACT.Identity, scale=rs[:, b, 2:3],
                                     bias=rs[:, b, 3:4]).then_inc(s_norm, 1)

            tiles(act, tile)

        @block.gpsimd
        def _(pool):
            pool.wait_ge(s_const, 32)

            def tile(i, b, r):
                pool.wait_ge(s_norm, i + 1)
                nc.gpsimd.tensor_tensor(z[:, b, :], z[:, b, :], lg[:], ALU.mult).then_inc(s_gain, 1)
                hold(pool, s_out, i + 1, s_passed)
                pool.dma_start(io["y"][bass.ds(i * P, P)], z[:, b, :]).then_inc(s_st[b], 16)

            tiles(pool, tile)
            for b in range(B):
                pool.wait_ge(s_st[b], 16 * (TILES // B + (1 if b == 0 else 0)))


def build(nc, io, ov_only=None):
    ctx = ExitStack()
    with ctx:
        ov = ctx.enter_context(nc.sbuf_tensor("further_blocks", [1, 2 * OVMAX + 1], I32))
        stage_attention(nc, io)
        stage_conv(nc, io)
        stage_dense(nc, io, ov)
        stage_experts(nc, io, ov)
        stage_norm(nc, io)


def kernel(x_prompt, x_sample, cache_k, cache_v, state_conv, w_in, attn_sinks, conv_w, g_attn_out, g_conv_out,
           w_out, ln1_g, ln1_b, router_w, router_bias, w_gate, w_up, w_down, ws_gate, ws_up, ws_down, ln2_g, ln2_b):
    import concourse.bacc as bacc
    from concourse.bass_utils import run_bass_kernel_spmd

    A = lambda a: np.asarray(a)
    C = np.ascontiguousarray
    xs = np.concatenate([A(x_prompt).reshape(SEQ, D), A(x_sample).reshape(NSAMP, D),
                         np.zeros((TPAD - T, D), np.float32)])
    rows = lambda w, n: C(A(w)[0].reshape(n, P, -1).transpose(1, 0, 2))
    sinks = A(attn_sinks)[0]
    srow = C(np.broadcast_to(sinks.reshape(KVH, 1, 1, GQ, 1), (KVH, 2, 4, GQ, DEC_S)).reshape(4, P).T)
    w_out_a = A(w_out)[0][:AW].reshape(KVH, GQ, HD, D).transpose(0, 2, 1, 3).reshape(P, GQ, D)
    w_out_c = A(w_out)[0][AW:].reshape(CC, P, D).transpose(1, 0, 2)
    data = {
        "xT": C(xs.reshape(TILES, P, KC, P).transpose(0, 3, 2, 1)), "x_rows": xs,
        "cache_k": A(cache_k)[0].reshape(DEC_B, P, KVH * HD), "cache_vn": A(cache_v)[0].reshape(DEC_B, P, KVH * HD),
        "cache_kT": C(A(cache_k)[0].reshape(2, 4, P, KVH * HD).transpose(3, 0, 1, 2).reshape(P, 2, 4 * P)),
        "cache_v": C(A(cache_v)[0].reshape(DEC_B, P, KVH * HD).transpose(1, 0, 2)),
        "state_conv": C(A(state_conv)[0].reshape(DEC_B, 2, CC, P).transpose(3, 2, 0, 1)),
        "w_in": rows(w_in, KC), "w_out": C(np.concatenate([w_out_a, w_out_c], 1)),
        "sinks": sinks, "srow": srow, "conv_w": C(A(conv_w)[0].reshape(3, CC, P).transpose(2, 1, 0)),
        "g_attn": C(A(g_attn_out)[0].reshape(KVH, GQ, HD).transpose(0, 2, 1).reshape(P, GQ)),
        "g_conv": C(A(g_conv_out)[0].reshape(CC, P).T),
        "ln1_g": A(ln1_g)[0], "ln1_b": A(ln1_b)[0], "ln2_g": A(ln2_g)[0], "ln2_b": A(ln2_b)[0],
        "router_w": rows(router_w, KC), "router_bias": A(router_bias)[0],
        "w_gate": A(w_gate)[0], "w_up": A(w_up)[0], "w_down": A(w_down)[0],
        "ws_gate": rows(ws_gate, KC), "ws_up": rows(ws_up, KC), "ws_down": rows(ws_down, FC),
    }
    data.update(shape_constants())
    nc = bacc.Bacc("TRN2", target_bir_lowering=False, num_devices=1)
    io, arrays = {}, {}
    for name, a in data.items():
        arrays[name] = C(a)
        io[name] = nc.dram_tensor(name, a.shape, mybir.dt.from_np(a.dtype), kind="ExternalInput").ap()
    outs = {"y": (TPAD, D), "kv_all": (TILES, P, 2, P), "ck_tail": (DEC_B, P - DEC_S, P), "cv_tail": (DEC_B, P - DEC_S, P),
            "conv_p": (P, CC, 2), "conv_s": (P, CC, DEC_B, 2)}
    for name, shape in outs.items():
        io[name] = nc.dram_tensor(name, shape, F32, kind="ExternalOutput").ap()
    inner = {"catA": ((TILES + 1, P, GQ, P), F32), "catC": ((TILES + 4, P, CC, P), F32), "ssA": ((P, TILES + 1), F32),
             "ssC": ((P, TILES), F32), "h_d": ((ROWS, D), F32), "acc_d": ((ROWS, D), F32), "table": ((SLOT_ROWS, 2), I32)}
    for name, (shape, dt) in inner.items():
        io[name] = nc.dram_tensor(name, shape, dt, kind="Internal").ap()
    build(nc, io)
    r = run_bass_kernel_spmd(nc, [arrays], core_ids=[0]).results[0]
    y, kv = r["y"], r["kv_all"]

    def window(n, tail):
        new = kv[TILES - 1, :NSAMP, n].reshape(DEC_B, DEC_S, P)
        return np.concatenate([r[tail], new], 1).reshape(1, DEC_B, P, KVH, HD)

    last = kv[PT_TILES - 1]
    return (y[:SEQ].reshape(1, SEQ, D), y[SEQ:T].reshape(DEC_B, DEC_S, D),
            C(last[:, 0]).reshape(1, 1, P, KVH, HD), C(last[:, 1]).reshape(1, 1, P, KVH, HD),
            C(r["conv_p"].transpose(2, 1, 0)).reshape(1, 1, 2, CH),
            window(0, "ck_tail"), window(1, "cv_tail"),
            C(r["conv_s"].transpose(2, 3, 1, 0)).reshape(1, DEC_B, 2, CH))
```

```python
from contextlib import ExitStack

import numpy as np
import concourse.bass as bass
from concourse import mybir

F32, F32R, BF16 = mybir.dt.float32, mybir.dt.float32r, mybir.dt.bfloat16
I32, U32 = mybir.dt.int32, mybir.dt.uint32
ACT = mybir.ActivationFunctionType
ALU = mybir.AluOpType
AX_X = mybir.AxisListType.X

P = 128
D = 1024
KC = D // P
SEQ, DEC_B, DEC_S, PAST = 2048, 8, 8, 8192
T = SEQ + DEC_B * DEC_S
PT_TILES = SEQ // P
TILES = PT_TILES + 1
TPAD = TILES * P
HEADS, KVH, HD, GQ = 8, 2, 64, 4
AW = HEADS * HD
QKV = AW + 2 * KVH * HD
ROT = HD // 4
CH = 512
CC = CH // P
NE, TOPK, FF = 64, 6, 256
FC = FF // P
NG, EPG, TOPG = 8, 8, 4
ALPHA = 2.0 ** 0.25
LN_EPS, RMS_EPS = 1e-5, 1e-6
NEG = -1.0e30
BIG = 3.0e38
BLK = 2 * P
SLOTS = 9 * BLK
TRASH_SLOT = NE * SLOTS
DROP_SLOT = TRASH_SLOT + BLK
SLOT_ROWS = DROP_SLOT + TOPK * P
ROWS = TPAD + P
OVMAX = 50
OVP = OVMAX // 2


def shape_constants():
    f = np.float32
    inv = (f(500000.0) ** (-np.arange(0, ROT, 2, dtype=f) / f(ROT))).astype(f)
    pos = np.concatenate([np.arange(SEQ), np.tile(PAST + np.arange(DEC_S), DEC_B), np.zeros(TPAD - T)]).astype(f)
    ang = (pos[:, None] * inv[None, :]).astype(f)
    c, s = np.cos(ang).astype(f), np.sin(ang).astype(f)
    rope = np.concatenate([c, c, -s, s], 1).reshape(TILES, P, 2 * ROT)
    r, k = np.arange(P)[:, None], np.arange(2 * P)[None, :]
    diff = r + P - k
    mask = np.where((diff >= 0) & (diff < P), f(0), f(NEG))
    mask0 = np.where(k < P, f(NEG), mask)
    row = np.arange(P)
    rb, rt = row // 32, row % 8
    cols = []
    for b in range(4):
        j = np.arange(P)[None, :]
        d = rt[:, None] + P - j
        cols.append((rb[:, None] == b) & (d >= 0) & (d < P))
    halves = []
    for half in range(2):
        new = [(rb[:, None] + 4 * half == b) & (rt[:, None] >= np.arange(DEC_S)[None, :]) for b in range(DEC_B)]
        halves.append(np.where(np.concatenate(cols + new, 1), f(0), f(NEG)))
    smask = np.stack(halves, 1)
    tok = np.arange(P)[:, None] + P * np.arange(TILES)[None, :]
    valid = (tok < T).astype(f)
    drop_to = DROP_SLOT + 1 + P * np.arange(TOPK)[None, None, :] + np.arange(P)[:, None, None]
    drop = ((1 - valid)[:, :, None] * drop_to).astype(f)
    e = np.arange(NE)
    base = np.broadcast_to(e * SLOTS + 1, (P, NE)).astype(f)
    tri = (np.arange(P)[:, None] < np.arange(P)[None, :]).astype(f)
    thr = np.broadcast_to(BLK * np.arange(1, 9), (NE, 8)).astype(f)
    nidx = np.broadcast_to(np.arange(OVMAX), (NE, OVMAX)).astype(f)
    ecol = np.stack([e, e * SLOTS + BLK - TRASH_SLOT, np.full(NE, BLK)], 1).astype(f)
    table0 = np.zeros((DROP_SLOT, 2), np.int32)
    table0[:, 0] = TPAD + np.arange(DROP_SLOT) % P
    return {
        "rope": rope.astype(f), "mask": np.stack([mask0, mask], 1).astype(f), "smask": smask.astype(f),
        "valid": valid, "drop": drop, "tokid": tok.astype(np.int32), "base": base.copy(),
        "tri": tri, "thr": thr.copy(), "nidx": nidx.copy(), "ecol": ecol,
        "table0": table0, "ident": np.eye(P, dtype=f),
    }


def hold(eng, sem, value, passed):
    eng.wait_ge(sem, value)
    eng.sem_inc(passed, 1)


class Phase:

    def __init__(self, nc, ctx, name):
        self.nc, self.ctx, self.name = nc, ctx, name

    def sb(self, name, shape, dt=F32):
        return self.ctx.enter_context(self.nc.sbuf_tensor(f"{self.name}_{name}", shape, dt))

    def ps(self, name, shape, dt=F32):
        return self.ctx.enter_context(self.nc.psum_tensor(f"{self.name}_{name}", shape, dt))

    def sem(self, name):
        return self.ctx.enter_context(self.nc.semaphore(f"{self.name}_{name}"))


def split_weights(nc, ph, pieces, raw):
    loaded = [ph.sem(f"wraw{b}") for b in range(2)]
    rounded, split = ph.sem("whi"), ph.sem("wlo")

    def raw_of(n):
        a, b = pieces[n][1].shape[1:]
        return raw[:, n % 2, 0:a * b].rearrange("p (a b) -> p a b", a=a)

    def sp_part(sp, first=0, end=len(pieces)):
        for n in range(first, end):
            src, hi, lo = pieces[n]
            if n >= 2:
                sp.wait_ge(split, n - 1)
            sp.dma_start(raw_of(n), src).then_inc(loaded[n % 2], 16)

    def act_part(act, first=0, end=len(pieces)):
        for n in range(first, end):
            src, hi, lo = pieces[n]
            act.wait_ge(loaded[n % 2], 16 * (n // 2 + 1))
            nc.scalar.activation(hi, raw_of(n), ACT.Copy).then_inc(rounded, 1)

    def dve_part(dve, first=0, end=len(pieces)):
        for n in range(first, end):
            src, hi, lo = pieces[n]
            dve.wait_ge(rounded, n + 1)
            nc.vector.tensor_tensor(lo, raw_of(n), hi.bitcast(F32), ALU.subtract).then_inc(split, 1)

    return sp_part, act_part, dve_part, split, len(pieces)


SK = 4 * P + DEC_B * DEC_S
NSAMP = DEC_B * DEC_S


def stage_attention(nc, io):
    with ExitStack() as ctx:
        ph = Phase(nc, ctx, "at")
        sb, ps, sem = ph.sb, ph.ps, ph.sem
        wh, wl = sb("wh", [P, KC, QKV], F32R), sb("wl", [P, KC, QKV], F32R)
        wraw = sb("wraw", [P, 2, QKV])
        xr = sb("xr", [P, KC, P])
        xh, xl = sb("xh", [P, KC, P], F32R), sb("xl", [P, KC, P], F32R)
        ident, ones = sb("ident", [P, P]), sb("ones", [P, 2])
        rope, mask = sb("rope", [P, 2 * ROT]), sb("mask", [P, 2, 2 * P])
        sinks, gat = sb("sinks", [P, HEADS]), sb("gat", [P, GQ])
        qk = sb("qk", [P, 10, HD])
        ra, rb = sb("ra", [P, 10, ROT]), sb("rb", [P, 10, ROT])
        qT = sb("qT", [P, GQ, P])
        kT = sb("kT", [P, 2 * P])
        vv = sb("vv", [P, 3, P])
        pr = sb("pr", [P, HEADS, 2 * P])
        pT = sb("pT", [P, KVH, 2, GQ, P])
        mx, ng = sb("mx", [P, HEADS]), sb("ng", [P, HEADS])
        dn, sk, rd = sb("dn", [P, HEADS]), sb("sk", [P, HEADS]), sb("rd", [P, HEADS])
        sq, cat = sb("sq", [P, GQ, P]), sb("cat", [P, GQ, P])
        ssa = sb("ssa", [P, TILES + 1])
        kcT = sb("kcT", [P, 2, SK])
        vc = sb("vc", [P, DEC_B, P])
        sm = sb("sm", [P, 2, SK])
        srow = sb("srow", [P, 4])
        spr = sb("spr", [P, 4, SK])
        spT = sb("spT", [P, 5, P])
        qTs = sb("qTs", [P, 2, P])

        psP = ps("psP", [P, 2, 512])
        psS = ps("psS", [P, HEADS, 2 * P])
        psT, psO = ps("psT", [P, 512]), ps("psO", [P, 512])

        s_const, s_samp, s_zero, s_passed = sem("const"), sem("sample_loaded"), sem("zero"), sem("passed")
        s_x, s_xh, s_xl, s_tab = sem("x_loaded"), sem("x_hi"), sem("x_lo"), sem("rope_loaded")
        s_proj, s_copied, s_rope = sem("projected"), sem("qkv_copied"), sem("roped")
        s_qkt, s_qkT = sem("qk_transposed"), sem("qkT_copied")
        s_score, s_max, s_exp, s_rd, s_prob = sem("scores"), sem("maxed"), sem("exped"), sem("rden"), sem("probs_pool")
        s_probd = sem("probs_dve")
        s_pT, s_pTa, s_pTd = sem("probsT"), sem("probsT_act"), sem("probsT_dve")
        s_pv, s_sq, s_cat, s_ss, s_sse = sem("pv"), sem("squared"), sem("cat"), sem("sumsq"), sem("sumsq_saved")
        s_st, s_shift, s_kvst = sem("stored"), sem("shifted"), sem("kv_stored")
        s_tail = sem("tail_out")
        s_g, s_ga, s_gp = sem("group_T"), sem("group_copied"), sem("group_pv")
        pieces = [(io["w_in"][:, kc:kc + 1, 0:QKV], wh[:, kc:kc + 1, :], wl[:, kc:kc + 1, :]) for kc in range(KC)]
        w_sp, w_act, w_dve, s_w, n_w = split_weights(nc, ph, pieces, wraw)
        consts = [(ident[:], io["ident"]), (mask[:], io["mask"]),
                  (sinks[:], io["sinks"].partition_broadcast(P)), (gat[:], io["g_attn"])]
        sample_in = [(sm[:], io["smask"]), (srow[:], io["srow"]), (vc[:], io["cache_v"]),
                  (kcT[:, 0, 0:4 * P], io["cache_kT"][:, 0]), (kcT[:, 1, 0:4 * P], io["cache_kT"][:, 1])]
        CONST, SAMPLE_IN = 16 * len(consts), 16 * len(sample_in)
        block = ctx.enter_context(nc.Block())

        @block.sync
        def _(sp):
            sp.dma_start(xr[:], io["xT"][0]).then_inc(s_x, 16)
            w_sp(sp, 0, 2)
            sp.dma_start(rope[:], io["rope"][0]).then_inc(s_tab, 16)
            for dst, src in consts:
                sp.dma_start(dst, src).then_inc(s_const, 16)
            w_sp(sp, 2)
            for dst, src in sample_in:
                sp.dma_start(dst, src).then_inc(s_samp, 16)

            def stores(i, load_next):
                if load_next:
                    sp.wait_ge(s_xl, i + 1)
                    sp.dma_start(xr[:], io["xT"][bass.ds(i + 1, 1)].rearrange("o p k t -> (o p) k t")).then_inc(s_x, 16)
                sp.wait_ge(s_rope, i + 1)
                if load_next:
                    sp.dma_start(rope[:], io["rope"][bass.ds(i + 1, 1)].rearrange("o p c -> (o p) c")).then_inc(s_tab, 16)
                sp.dma_start(io["kv_all"][bass.ds(i, 1), :, 0].rearrange("o p c -> (o p) c"),
                             qk[:, 8:10, :].rearrange("p h d -> p (h d)")).then_inc(s_kvst, 16)
                sp.dma_start(io["kv_all"][bass.ds(i, 1), :, 1].rearrange("o p c -> (o p) c"),
                             vv[:, 2, :]).then_inc(s_kvst, 16)
                sp.wait_ge(s_cat, i + 1)
                sp.dma_start(io["catA"][bass.ds(i, 1)].rearrange("o p k t -> (o p) k t"), cat[:]).then_inc(s_st, 16)

            with sp.Fori(0, PT_TILES) as i:
                stores(i, True)
            stores(PT_TILES, False)
            sp.wait_ge(s_cat, TILES + 1)
            sp.dma_start(io["catA"][TILES], cat[:]).then_inc(s_st, 16)
            sp.wait_ge(s_sse, TILES + 1)
            sp.dma_start(io["ssA"], ssa[:]).then_inc(s_st, 16)
            sp.wait_ge(s_st, 16 * (TILES + 2))
            sp.wait_ge(s_kvst, 32 * TILES)

        @block.gpsimd
        def _(pool):
            for buf in (pr, kT, ones, vv):
                nc.gpsimd.memset(buf[:], 1.0 if buf is ones else 0.0).then_inc(s_zero, 1)
            pool.dma_start(io["ck_tail"], io["cache_k"][:, DEC_S:]).then_inc(s_tail, 16)
            pool.dma_start(io["cv_tail"], io["cache_vn"][:, DEC_S:]).then_inc(s_tail, 16)
            pool.wait_ge(s_zero, 4)

            def shift(i):
                hold(pool, s_pv, i, s_passed)
                hold(pool, s_kvst, 32 * i, s_passed)
                nc.gpsimd.tensor_copy(vv[:, 0, :], vv[:, 1, :])
                pool.drain()
                nc.gpsimd.tensor_copy(vv[:, 1, :], vv[:, 2, :])
                hold(pool, s_score, 2 * i, s_passed)
                nc.gpsimd.tensor_copy(kT[:, 0:P], kT[:, P:2 * P])
                pool.drain().then_inc(s_shift, 1)

            with pool.Fori(0, PT_TILES) as i:
                shift(i)
                pool.wait_ge(s_rd, i + 1)
                nc.gpsimd.tensor_tensor(pr[:, 0:GQ], pr[:, 0:GQ], rd[:, 0:GQ].unsqueeze(2).to_broadcast([P, GQ, 2 * P]),
                                        ALU.mult).then_inc(s_prob, 1)
            shift(PT_TILES)
            pool.wait_ge(s_rd, TILES)
            nc.gpsimd.tensor_tensor(spr[:], spr[:], rd[:, 0:4].unsqueeze(2).to_broadcast([P, 4, SK]),
                                    ALU.mult).then_inc(s_prob, 1)
            pool.wait_ge(s_tail, 32)

        @block.scalar
        def _(act):
            act.wait_ge(s_x, 16)
            nc.scalar.activation(xh[:], xr[:], ACT.Copy).then_inc(s_xh, 1)
            w_act(act)
            act.wait_ge(s_const, CONST)
            act.wait_ge(s_zero, 4)

            def copy_probs(i):
                act.wait_ge(s_pT, i + 1)
                act.wait_ge(s_pv, i)
                nc.scalar.activation(pT[:, 0].rearrange("p h g q -> p (h g q)"),
                                     psS[:, 0:4].rearrange("p h q -> p (h q)"), ACT.Copy).then_inc(s_pTa, 1)

            def projected(i):
                act.wait_ge(s_proj, i + 1)
                act.wait_ge(s_shift, i + 1)
                act.wait_ge(s_kvst, 32 * i)
                act.wait_ge(s_qkt, i)
                for kv in range(KVH):
                    nc.scalar.activation(qk[:, kv:8:2, :], psP[:, 0, kv * 256:(kv + 1) * 256].rearrange("p (g d) -> p g d", g=GQ), ACT.Copy)
                nc.scalar.activation(qk[:, 8:10, :].rearrange("p h d -> p (h d)"), psP[:, 1, 0:P], ACT.Copy)
                nc.scalar.activation(vv[:, 2, :], psP[:, 1, P:2 * P], ACT.Copy).then_inc(s_copied, 1)

            def copy_qkT(i):
                act.wait_ge(s_qkt, i + 1)
                act.wait_ge(s_score, 2 * i)
                nc.scalar.activation(qT[:].rearrange("p g q -> p (g q)"), psT[:], ACT.Copy)
                nc.scalar.activation(kT[:, P:2 * P], psP[:, 1, 256:384], ACT.Copy).then_inc(s_qkT, 1)

            def squares(n):
                act.wait_ge(s_pv, n + 1)
                act.wait_ge(s_ss, n)
                nc.scalar.activation(sq[:].rearrange("p g q -> p (g q)"), psO[:], ACT.Square).then_inc(s_sq, 1)

            def save(n):
                act.wait_ge(s_ss, n + 1)
                nc.scalar.activation(ssa[:, bass.ds(n, 1)], psP[:, 1, 384:385], ACT.Copy).then_inc(s_sse, 1)

            with act.Fori(0, PT_TILES) as i:
                copy_probs(i)
                projected(i)
                act.wait_ge(s_x, 16 * (i + 2))
                nc.scalar.activation(xh[:], xr[:], ACT.Copy).then_inc(s_xh, 1)
                squares(i)
                copy_qkT(i)
                save(i)
                for half in range(2):
                    act.wait_ge(s_max, 2 * i + half + 1)
                    for h in range(half * GQ, half * GQ + GQ):
                        nc.scalar.activation(pr[:, h, :], pr[:, h, :], ACT.Exp, bias=ng[:, h:h + 1],
                                             accum_out=dn[:, h:h + 1])
                    nc.scalar.activation(sk[:, half * GQ:half * GQ + GQ], sk[:, half * GQ:half * GQ + GQ], ACT.Exp).then_inc(s_exp, 1)
            copy_probs(PT_TILES)
            projected(PT_TILES)
            squares(PT_TILES)
            copy_qkT(PT_TILES)
            act.wait_ge(s_samp, SAMPLE_IN)
            act.wait_ge(s_qkT, TILES)
            for half in range(2):
                for g in range(GQ):
                    nc.scalar.activation(qTs[:, half].rearrange("p (b g t) -> p g b t", b=4, g=GQ)[:, g],
                                         qT[:, g, half * 32:half * 32 + 32].rearrange("p (b t) -> p b t", b=4), ACT.Copy)
                nc.scalar.activation(kcT[:, half, 4 * P:SK], kT[:, P:P + NSAMP], ACT.Copy)
            act.drain().then_inc(s_ga, 1)
            act.wait_ge(s_max, 2 * TILES)
            for n in range(4):
                nc.scalar.activation(spr[:, n, :], spr[:, n, :], ACT.Exp, bias=ng[:, n:n + 1],
                                     accum_out=dn[:, n:n + 1])
            nc.scalar.activation(sk[:, 0:4], sk[:, 0:4], ACT.Exp).then_inc(s_exp, 2)
            save(PT_TILES)
            for n in range(4):
                act.wait_ge(s_g, n + 1)
                nc.scalar.activation(spT[:, 0:4, :].rearrange("p b r -> p (b r)"), psT[:], ACT.Copy)
                nc.scalar.activation(spT[0:NSAMP, 4, :], psS[0:NSAMP, 0, 0:P], ACT.Copy).then_inc(s_ga, 1)
            act.wait_ge(s_gp, 4)
            act.wait_ge(s_ss, TILES)
            for half in range(2):
                last = nc.scalar.activation(sq[:, half].rearrange("p (g b t) -> p b g t", b=4, g=GQ),
                                            psO[:, half * P:(half + 1) * P].rearrange("p (b g t) -> p b g t", b=4, g=GQ), ACT.Square)
            last.then_inc(s_sq, 1)
            save(TILES)

        @block.vector
        def _(dve):
            dve.wait_ge(s_xh, 1)
            nc.vector.tensor_tensor(xl[:], xr[:], xh[:].bitcast(F32), ALU.subtract).then_inc(s_xl, 1)
            w_dve(dve)
            nc.vector.memset(cat[:], 0.0)
            nc.vector.memset(ssa[:], 0.0)
            dve.wait_ge(s_const, CONST)
            dve.wait_ge(s_zero, 4)

            def rotate(i):
                dve.wait_ge(s_copied, i + 1)
                dve.wait_ge(s_tab, 16 * (i + 1))
                nc.vector.tensor_tensor(ra[:], qk[:, :, 0:ROT], rope[:, 0:ROT].unsqueeze(1).to_broadcast([P, 10, ROT]), ALU.mult)
                nc.vector.tensor_tensor(rb[:, :, 0:8], qk[:, :, 8:16], rope[:, ROT:ROT + 8].unsqueeze(1).to_broadcast([P, 10, 8]), ALU.mult)
                nc.vector.tensor_tensor(rb[:, :, 8:16], qk[:, :, 0:8], rope[:, ROT + 8:2 * ROT].unsqueeze(1).to_broadcast([P, 10, 8]), ALU.mult)
                dve.drain()
                nc.vector.tensor_tensor(qk[:, :, 0:ROT], ra[:], rb[:], ALU.add).then_inc(s_rope, 1)

            def copy_probs(i):
                dve.wait_ge(s_pT, i + 1)
                dve.wait_ge(s_pv, i)
                nc.vector.tensor_copy(pT[:, 1].rearrange("p h g q -> p (h g q)"),
                                      psS[:, 4:8].rearrange("p h q -> p (h q)")).then_inc(s_pTd, 1)

            def features(n):
                dve.wait_ge(s_sq, n + 1)
                dve.wait_ge(s_st, 16 * n)
                nc.vector.tensor_tensor(cat[:], psO[:].rearrange("p (g q) -> p g q", g=GQ),
                                        gat[:].unsqueeze(2).to_broadcast([P, GQ, P]), ALU.mult).then_inc(s_cat, 1)

            def softmax_max(view, cols, snk, amount):
                dve.drain()
                nc.vector.tensor_reduce(mx[:, cols], view, AX_X, ALU.max)
                dve.drain()
                nc.vector.tensor_tensor(mx[:, cols], mx[:, cols], snk, ALU.max)
                dve.drain()
                nc.vector.tensor_scalar(ng[:, cols], mx[:, cols], -1.0, None, ALU.mult)
                nc.vector.tensor_tensor(sk[:, cols], snk, mx[:, cols], ALU.subtract)
                dve.drain().then_inc(s_max, amount)

            def denominators(count, cols):
                dve.wait_ge(s_exp, count)
                nc.vector.tensor_tensor(dn[:, cols], dn[:, cols], sk[:, cols], ALU.add)
                dve.drain()
                return nc.vector.reciprocal(rd[:, cols], dn[:, cols])

            HALF = (slice(0, GQ), slice(GQ, HEADS))
            with dve.Fori(0, PT_TILES) as i:
                copy_probs(i)
                rotate(i)
                dve.wait_ge(s_xh, i + 2)
                dve.wait_ge(s_proj, i + 1)
                nc.vector.tensor_tensor(xl[:], xr[:], xh[:].bitcast(F32), ALU.subtract).then_inc(s_xl, 1)
                features(i)
                dve.wait_ge(s_pT, i + 1)
                for half in range(2):
                    dve.wait_ge(s_score, 2 * i + half + 1)
                    for b in range(2 * half, 2 * half + 2):
                        nc.vector.scalar_tensor_tensor(pr[:, 2 * b:2 * b + 2, :], psS[:, 2 * b:2 * b + 2, :], HD ** -0.5,
                                                       mask[:, 0, :].unsqueeze(1).to_broadcast([P, 2, 2 * P]),
                                                       ALU.mult, ALU.add)
                    softmax_max(pr[:, HALF[half]], HALF[half], sinks[:, HALF[half]], 1)
                nc.vector.tensor_copy(mask[:, 0, :], mask[:, 1, :])
                denominators(2 * i + 1, HALF[0]).then_inc(s_rd, 1)
                denominators(2 * i + 2, HALF[1])
                dve.drain()
                nc.vector.tensor_tensor(pr[:, HALF[1]], pr[:, HALF[1]], rd[:, HALF[1]].unsqueeze(2).to_broadcast([P, GQ, 2 * P]),
                                        ALU.mult).then_inc(s_probd, 1)
            copy_probs(PT_TILES)
            rotate(PT_TILES)
            features(PT_TILES)
            dve.wait_ge(s_samp, SAMPLE_IN)
            dve.wait_ge(s_score, 2 * TILES)
            for n in range(4):
                half, new = n % 2, psT if n < 2 else psP[:, 0]
                nc.vector.scalar_tensor_tensor(spr[:, n, 0:4 * P], psS[:, 2 * n:2 * n + 2].rearrange("p h q -> p (h q)"),
                                               HD ** -0.5, sm[:, half, 0:4 * P], ALU.mult, ALU.add)
                nc.vector.scalar_tensor_tensor(spr[:, n, 4 * P:SK], new[:, half * NSAMP:(half + 1) * NSAMP],
                                               HD ** -0.5, sm[:, half, 4 * P:SK], ALU.mult, ALU.add)
            softmax_max(spr[:], slice(0, 4), srow[:], 2)
            denominators(2 * TILES, slice(0, 4)).then_inc(s_rd, 1)
            dve.wait_ge(s_sq, TILES + 1)
            dve.wait_ge(s_st, 16 * TILES)
            nc.vector.memset(cat[:, :, NSAMP:P], 0.0)
            for half in range(2):
                for g in range(GQ):
                    nc.vector.tensor_scalar(cat[:, g, half * 32:half * 32 + 32].rearrange("p (b t) -> p b t", b=4),
                                            psO[:, half * P:(half + 1) * P].rearrange("p (b g t) -> p g b t", b=4, g=GQ)[:, g],
                                            gat[:, g:g + 1], None, ALU.mult)
            dve.drain().then_inc(s_cat, 1)

        @block.tensor
        def _(pe):
            pe.wait_ge(s_zero, 4)

            def project(i):
                pe.wait_ge(s_xl, i + 1)
                pe.wait_ge(s_copied, i)
                pe.wait_ge(s_qkT, i)
                pe.wait_ge(s_sse, i)
                FIRST = 7
                multiply(range(FIRST))
                pe.wait_ge(s_const, CONST)
                pe.wait_ge(s_prob, i)
                pe.wait_ge(s_probd, i)
                for kv in range(KVH):
                    for half in range(2):
                        for g in range(GQ):
                            last = nc.tensor.transpose(
                                psS[:, 4 * kv + 2 * half + g // 2, (g % 2) * P:(g % 2 + 1) * P],
                                pr[:, 4 * kv + g, half * P:(half + 1) * P], ident[:])
                last.then_inc(s_pT, 1)
                multiply(range(FIRST, KC)).then_inc(s_proj, 1)

            def multiply(chunks):
                for kc in chunks:
                    pe.wait_ge(s_w, kc + 1)
                    for n, (a, b) in enumerate(((xh, wh), (xh, wl), (xl, wh))):
                        for j, (lo, hi) in enumerate(((0, 512), (512, QKV))):
                            last = nc.tensor.matmul(psP[:, j, 0:hi - lo], a[:, kc, :], b[:, kc, lo:hi],
                                                    start=(kc == 0 and n == 0), stop=(kc == KC - 1 and n == 2))
                return last

            def transpose_qk(i):
                pe.wait_ge(s_rope, i + 1)
                for g in range(GQ):
                    nc.tensor.transpose(psT[:, g * P:(g + 1) * P],
                                        qk[:, 2 * g:2 * g + 2, :].rearrange("p h d -> p (h d)"), ident[:])
                nc.tensor.transpose(psP[:, 1, 256:384], qk[:, 8:10, :].rearrange("p h d -> p (h d)"),
                                    ident[:]).then_inc(s_qkt, 1)

            def values(n):
                pe.wait_ge(s_pTa, n + 1)
                pe.wait_ge(s_pTd, n + 1)
                pe.wait_ge(s_cat, n)
                pe.wait_ge(s_sq, n)
                pe.wait_ge(s_shift, n + 1)
                for kv in range(KVH):
                    for half in range(2):
                        last = nc.tensor.matmul(psO[kv * HD:(kv + 1) * HD, :], vv[:, half, kv * HD:(kv + 1) * HD],
                                                pT[:, kv, half].rearrange("p g q -> p (g q)"),
                                                start=(half == 0), stop=(half == 1))
                last.then_inc(s_pv, 1)

            def sum_squares(n, lhs):
                pe.wait_ge(s_sq, n + 1)
                pe.wait_ge(s_sse, n)
                for j, l in enumerate(lhs):
                    last = nc.tensor.matmul(psP[:, 1, 384:385], l, ones[:, 0:1], start=(j == 0), stop=(j == len(lhs) - 1))
                last.then_inc(s_ss, 1)

            with pe.Fori(0, PT_TILES) as i:
                project(i)
                values(i)
                transpose_qk(i)
                pe.wait_ge(s_qkT, i + 1)
                for kv in range(KVH):
                    for g in range(GQ):
                        last = nc.tensor.matmul(psS[:, kv * GQ + g, :], qT[kv * HD:(kv + 1) * HD, g, :],
                                                kT[kv * HD:(kv + 1) * HD, :], start=True, stop=True)
                    last.then_inc(s_score, 1)
                    if kv == 0:
                        sum_squares(i, [sq[:, g, :] for g in range(GQ)])
            project(PT_TILES)
            values(PT_TILES)
            transpose_qk(PT_TILES)
            pe.wait_ge(s_qkT, TILES)
            sum_squares(PT_TILES, [sq[:, g, :] for g in range(GQ)])
            pe.wait_ge(s_samp, SAMPLE_IN)
            pe.wait_ge(s_ga, 1)
            for n in range(4):
                kv, half = n // 2, n % 2
                lhs = qTs[kv * HD:(kv + 1) * HD, half, :]
                nc.tensor.matmul(psS[:, 2 * n:2 * n + 2].rearrange("p h q -> p (h q)"), lhs,
                                 kcT[kv * HD:(kv + 1) * HD, half, 0:4 * P], start=True, stop=True)
                new = psT if kv == 0 else psP[:, 0]
                last = nc.tensor.matmul(new[:, half * NSAMP:(half + 1) * NSAMP], lhs,
                                        kcT[kv * HD:(kv + 1) * HD, half, 4 * P:SK], start=True, stop=True)
            last.then_inc(s_score, 2)
            pe.wait_ge(s_prob, TILES)
            pe.wait_ge(s_cat, TILES)
            pe.wait_ge(s_sq, TILES)
            for n in range(4):
                kv, half = n // 2, n % 2
                pe.wait_ge(s_ga, n + 1)
                for b in range(4):
                    nc.tensor.transpose(psT[:, b * P:(b + 1) * P], spr[:, n, b * P:(b + 1) * P], ident[:])
                nc.tensor.transpose(psS[0:NSAMP, 0, 0:P], spr[:, n, 4 * P:SK], ident[:]).then_inc(s_g, 1)
                pe.wait_ge(s_ga, n + 2)
                out = psO[kv * HD:(kv + 1) * HD, half * P:(half + 1) * P]
                for b in range(4):
                    nc.tensor.matmul(out, vc[:, 4 * half + b, kv * HD:(kv + 1) * HD], spT[:, b, :],
                                     start=(b == 0), stop=False)
                nc.tensor.matmul(out, vv[0:NSAMP, 2, kv * HD:(kv + 1) * HD], spT[0:NSAMP, 4, :],
                                 start=False, stop=True).then_inc(s_gp, 1)
            pe.wait_ge(s_sq, TILES + 1)
            pe.wait_ge(s_sse, TILES)
            for half in range(2):
                for g in range(GQ):
                    last = nc.tensor.matmul(psP[half * 32:half * 32 + 32, 1, 384:385],
                                            sq[:, half, g * 32:(g + 1) * 32],
                                            ones[:, 0:1], start=(g == 0), stop=(g == GQ - 1))
            last.then_inc(s_ss, 1)


def stage_conv(nc, io):
    N = 4 * P
    STEPS = SEQ // N
    SETS = 2
    with ExitStack() as ctx:
        ph = Phase(nc, ctx, "cv")
        sb, ps, sem = ph.sb, ph.ps, ph.sem
        wh, wl = sb("wh", [P, KC, 3 * CH], F32R), sb("wl", [P, KC, 3 * CH], F32R)
        xr = sb("xr", [P, 4, KC, P])
        xh, xl = sb("xh", [P, 2, KC, N], F32R), sb("xl", [P, 2, KC, N], F32R)
        gated = sb("gated", [P, CC, N + 2])
        gs = sb("gs", [P, CC, DEC_B, DEC_S + 2])
        us, tmp = sb("us", [P, N]), sb("tmp", [P, N])
        sq, ss = sb("sq", [P, 2, N]), sb("ss", [P, N])
        cat = sb("cat", [P, 4, CC, P])
        ones, cw, gcv = sb("ones", [P, 2]), sb("cw", [P, CC, 3]), sb("gcv", [P, CC])
        ssc = sb("ssc", [P, TILES + 7])
        psG = ps("psG", [P, SETS, 3, 512])
        psQ = ps("psQ", [P, 512])

        s_const, s_x, s_xh, s_xl = sem("const"), sem("x_loaded"), sem("x_hi"), sem("x_lo")
        s_x0_loaded, s_x0 = [sem(f"first_x_loaded{a}") for a in range(4)], sem("first_x_hi")
        s_proj, s_u, s_gate, s_tap = (sem(n) for n in ("projected", "u_copied", "gated", "tap0"))
        s_conv = sem("conv_or_free")
        s_sq, s_sum, s_cat, s_ss, s_sse, s_st, s_zero = (sem(n) for n in ("squared", "chunks_summed", "cat", "sumsq", "sumsq_saved", "stored", "zero"))
        ident = sb("ident", [P, P])
        s_rows, s_rowsc = sem("sample_rows"), sem("sample_rows_copied")
        CONST = 64
        rowmajor = xr[0:NSAMP].rearrange("p a k t -> p a (k t)")[:, 0:3, 0:CH]
        raw = cat[:].rearrange("p a c t -> p (a c t)").rearrange("p (b n) -> p b n", b=2)
        ORDER = (0, 2, 1)
        pieces = []
        for c in range(CC):
            for col in ORDER:
                at = slice(col * CH + c * P, col * CH + (c + 1) * P)
                pieces.append((io["w_in"][:, :, QKV + col * CH + c * P:QKV + col * CH + (c + 1) * P], wh[:, :, at], wl[:, :, at]))
        w_sp, w_act, w_dve, s_w, n_w = split_weights(nc, ph, pieces, raw)
        block = ctx.enter_context(nc.Block())

        def steps(eng, step):
            with eng.Fori(0, STEPS // 2) as j:
                step(2 * j, 0)
                step(2 * j + 1, 1)

        @block.sync
        def _(sp):
            for a in range(4):
                sp.dma_start(xr[:, a], io["xT"][a]).then_inc(s_x0_loaded[a], 16)
            w_sp(sp)
            sp.wait_ge(s_w, n_w)

            def step(i, k):
                sp.wait_ge(s_cat, CC * i)
                sp.dma_start(io["catC"][bass.ds(4 * i, 4)].rearrange("a p k t -> p a k t"), cat[:]).then_inc(s_st, 16)
                sp.wait_ge(s_xl, i + 1)
                sp.dma_start(xr[:], io["xT"][bass.ds(4 * i + 4, 4)].rearrange("a p k t -> p a k t")).then_inc(s_x, 16)

            steps(sp, step)
            sp.wait_ge(s_cat, CC * STEPS)
            sp.dma_start(io["catC"][bass.ds(4 * STEPS, 4)].rearrange("a p k t -> p a k t"), cat[:]).then_inc(s_st, 16)
            with nc.allow_non_contiguous_dma(reason="two columns of the state"):
                sp.wait_ge(s_cat, CC * (STEPS + 1))
                sp.dma_start(io["conv_p"], gated[:, :, 0:2]).then_inc(s_st, 16)
                sp.dma_start(io["conv_s"], gs[:, :, :, DEC_S:DEC_S + 2]).then_inc(s_st, 16)
            sp.dma_start(io["catC"][4 + PT_TILES], cat[:, 0]).then_inc(s_st, 16)
            sp.wait_ge(s_sse, STEPS + 2)
            sp.dma_start(io["ssC"], ssc[:]).then_inc(s_st, 16)
            sp.wait_ge(s_st, 16 * (STEPS + 5))

        @block.gpsimd
        def _(pool):
            pool.dma_start(cw[:], io["conv_w"]).then_inc(s_const, 16)
            pool.dma_start(gcv[:], io["g_conv"]).then_inc(s_const, 16)
            pool.dma_start(gs[:, :, :, 0:2], io["state_conv"]).then_inc(s_const, 16)
            pool.dma_start(ident[:], io["ident"]).then_inc(s_const, 16)

            def sum_chunks(i):
                pool.wait_ge(s_sq, CC * i + 2)
                pool.wait_ge(s_ss, i + 1)
                nc.gpsimd.tensor_tensor(ss[:], sq[:, 0, :], sq[:, 1, :], ALU.add).then_inc(s_sum, 1)
                for c in (2, 3):
                    pool.wait_ge(s_sq, CC * i + c + 1)
                    pool.wait_ge(s_sum, (CC - 1) * i + c - 1)
                    nc.gpsimd.tensor_tensor(ss[:], ss[:], sq[:, c % 2, :], ALU.add).then_inc(s_sum, 1)

            pool.wait_ge(s_zero, 1)
            with pool.Fori(0, STEPS) as i:
                sum_chunks(i)
            sum_chunks(STEPS)

        @block.scalar
        def _(act):
            def round_x(i, k):
                act.wait_ge(s_x, 16 * i)
                nc.scalar.activation(xh[:, k].rearrange("p k (a t) -> p a k t", a=4), xr[:], ACT.Copy).then_inc(s_xh, 1)

            def chunk(i, c, u, cols, g, grid, out):
                m = CC * i + c
                act.wait_ge(s_proj, 3 * m + 1)
                act.wait_ge(s_gate, m)
                nc.scalar.activation(us[:, 0:u.shape[1]], u, ACT.Copy).then_inc(s_u, 1)
                act.wait_ge(s_gate, m + 1)
                act.wait_ge(s_conv, SETS + m)
                nc.scalar.activation(g(tmp), grid(0), ACT.Copy, scale=cw[:, c, 0:1]).then_inc(s_tap, 1)
                act.wait_ge(s_conv, SETS + m + 1)
                act.wait_ge(s_sum, (CC - 1) * i + (1 if c >= 2 else 0))
                nc.scalar.activation(sq[:, c % 2, 0:cols], tmp[:, 0:cols], ACT.Square).then_inc(s_sq, 1)
                if c == 0:
                    act.wait_ge(s_st, 16 * (i + 1))
                nc.scalar.activation(out, tmp[:, 0:cols], ACT.Copy, scale=gcv[:, c:c + 1]).then_inc(s_cat, 1)

            def save(n):
                act.wait_ge(s_ss, n + 1)
                nc.scalar.activation(ssc[:, bass.ds(4 * n, 4)], psQ[:, 0:4], ACT.Copy).then_inc(s_sse, 1)

            for a in range(4):
                act.wait_ge(s_x0_loaded[a], 16)
                nc.scalar.activation(xh[:, 0, :, a * P:(a + 1) * P], xr[:, a], ACT.Copy).then_inc(s_x0, 1)
            w_act(act)
            act.wait_ge(s_const, CONST)
            act.wait_ge(s_zero, 1)

            def step(i, k):
                for c in range(CC):
                    chunk(i, c, psG[:, c % SETS, 0, :], N, lambda t: t[:], lambda q: gated[:, c, q:q + N], cat[:, :, c, :])
                    if c == 1:
                        round_x(i + 1, 1 - k)
                    if c == 2:
                        save(i)

            steps(act, step)
            save(STEPS)
            act.wait_ge(s_xl, STEPS + 1)
            for j in range(3):
                act.wait_ge(s_rows, j + 1)
                nc.scalar.activation(rowmajor[:, j, :], psG[0:NSAMP, 0, j, :], ACT.Copy).then_inc(s_rowsc, 1)
            for c in range(CC):
                chunk(STEPS, c, psG[:, 1, 0, c * NSAMP:(c + 1) * NSAMP], P, lambda t: t[:, 0:NSAMP].rearrange("p (b t) -> p b t", b=DEC_B),
                      lambda q: gs[:, c, :, q:q + DEC_S], cat[:, 0, c, :])
            save(STEPS + 1)

        @block.vector
        def _(dve):
            def split_x(i, k):
                dve.wait_ge(s_xh, i)
                nc.vector.tensor_tensor(xl[:, k].rearrange("p k (a t) -> p a k t", a=4), xr[:],
                                        xh[:, k].bitcast(F32).rearrange("p k (a t) -> p a k t", a=4),
                                        ALU.subtract).then_inc(s_xl, 1)

            nc.vector.memset(gated[:], 0.0)
            nc.vector.memset(tmp[:], 0.0)
            nc.vector.memset(sq[:], 0.0)
            nc.vector.memset(ss[:], 0.0)
            nc.vector.memset(ones[:], 1.0)
            dve.drain().then_inc(s_zero, 1)
            dve.drain().then_inc(s_conv, SETS)
            for a in range(4):
                dve.wait_ge(s_x0, a + 1)
                last = nc.vector.tensor_tensor(xl[:, 0, :, a * P:(a + 1) * P], xr[:, a], xh[:, 0, :, a * P:(a + 1) * P].bitcast(F32), ALU.subtract)
            last.then_inc(s_xl, 1)
            w_dve(dve)
            dve.wait_ge(s_const, CONST)

            def chunk(i, c, view, C, B, mid, grid):
                m = CC * i + c
                dve.wait_ge(s_u, m + 1)
                dve.wait_ge(s_proj, 3 * m + 2)
                nc.vector.tensor_tensor(mid, C, view(us), ALU.mult).then_inc(s_gate, 1)
                dve.wait_ge(s_tap, m + 1)
                nc.vector.scalar_tensor_tensor(view(tmp), grid(1), cw[:, c, 1:2], view(tmp), ALU.mult, ALU.add)
                dve.drain()
                nc.vector.scalar_tensor_tensor(view(tmp), grid(2), cw[:, c, 2:3], view(tmp), ALU.mult, ALU.add)
                dve.drain()
                dve.wait_ge(s_proj, 3 * m + 3)
                nc.vector.tensor_tensor(view(tmp), view(tmp), B, ALU.mult).then_inc(s_conv, 1)

            def step(i, k):
                for c in range(CC):
                    chunk(i, c, lambda t: t[:, 0:N], psG[:, c % SETS, 1, :], psG[:, c % SETS, 2, :], gated[:, c, 2:N + 2], lambda q: gated[:, c, q:q + N])
                    if c == 1:
                        split_x(i + 1, 1 - k)
                dve.drain()
                nc.vector.tensor_copy(gated[:, :, 0:2], gated[:, :, N:N + 2])
                dve.drain()

            steps(dve, step)
            samp = lambda t: t[:, 0:NSAMP].rearrange("p (b t) -> p b t", b=DEC_B)
            for c in range(CC):
                C, B = (psG[:, 1, j, c * NSAMP:(c + 1) * NSAMP].rearrange("p (b t) -> p b t", b=DEC_B) for j in (1, 2))
                chunk(STEPS, c, samp, C, B, gs[:, c, :, 2:DEC_S + 2], lambda q: gs[:, c, :, q:q + DEC_S])

        @block.tensor
        def _(pe):
            def chunk(i, c, k):
                pe.wait_ge(s_conv, CC * i + c + 1)
                for j, col in enumerate(ORDER):
                    pe.wait_ge(s_w, 3 * c + j + 1)
                    for kc in range(KC):
                        for q, (a, b) in enumerate(((wh, xh), (wh, xl), (wl, xh))):
                            last = nc.tensor.matmul(psG[:, c % SETS, j, :],
                                                    a[:, kc, col * CH + c * P:col * CH + (c + 1) * P],
                                                    b[:, k, kc, :], start=(kc == 0 and q == 0),
                                                    stop=(kc == KC - 1 and q == 2))
                    last.then_inc(s_proj, 1)

            def sums(n):
                pe.wait_ge(s_sum, (CC - 1) * n)
                pe.wait_ge(s_sse, n)
                for a in range(4):
                    last = nc.tensor.matmul(psQ[:, a:a + 1], ss[:, a * P:(a + 1) * P], ones[:, 0:1], start=True, stop=True)
                last.then_inc(s_ss, 1)

            def step(i, k):
                pe.wait_ge(s_xl, i + 1)
                for c in range(CC):
                    chunk(i, c, k)
                    if c == 1:
                        sums(i)

            pe.wait_ge(s_zero, 1)
            steps(pe, step)
            sums(STEPS)
            pe.wait_ge(s_xl, STEPS + 1)
            pe.wait_ge(s_const, CONST)
            pe.wait_ge(s_conv, CC * STEPS + 1)
            for j, col in enumerate(ORDER):
                for kc in range(KC):
                    for q, (a, b) in enumerate(((xh, wh), (xh, wl), (xl, wh))):
                        last = nc.tensor.matmul(psG[0:NSAMP, 0, j, :], a[:, 0, kc, 0:NSAMP],
                                                b[:, kc, col * CH:(col + 1) * CH], start=(kc == 0 and q == 0),
                                                stop=(kc == KC - 1 and q == 2))
                last.then_inc(s_rows, 1)
            pe.wait_ge(s_conv, CC * STEPS + 2)
            for j in range(3):
                pe.wait_ge(s_rowsc, j + 1)
                for c in range(CC):
                    last = nc.tensor.transpose(psG[:, 1, j, c * NSAMP:(c + 1) * NSAMP],
                                               rowmajor[:, j, c * P:(c + 1) * P], ident[0:NSAMP, 0:NSAMP])
            last.then_inc(s_proj, 3 * CC)
            sums(STEPS + 1)


def stage_dense(nc, io, ov):
    with ExitStack() as ctx:
        ph = Phase(nc, ctx, "de")
        sb, ps, sem = ph.sb, ph.ps, ph.sem
        woh, wol = sb("woh", [P, KC, D], F32R), sb("wol", [P, KC, D], F32R)
        guh, gul = sb("guh", [P, KC, 2 * FF], F32R), sb("gul", [P, KC, 2 * FF], F32R)
        dnh, dnl = sb("dnh", [P, FC, D], F32R), sb("dnl", [P, FC, D], F32R)
        rw = sb("rw", [P, KC, 2 * NE], F32R)
        eye2, lt = sb("eye2", [P, NE]), sb("lt", [P, 2 * P])
        cr = sb("cr", [P, KC, P])
        ch, cl = sb("ch", [P, KC, P], F32R), sb("cl", [P, KC, P], F32R)
        hT = sb("hT", [P, KC, 2, P], F32R)
        xr, t = sb("xr", [P, D]), sb("t", [P, D])
        raw = sb("raw", [P, 2, 2 * D])
        h = sb("h", [P, 2, D])
        acc = sb("acc", [P, D])
        lg, lb = sb("lg", [P, D]), sb("lb", [P, D])
        ident, ones = sb("ident", [P, P]), sb("ones", [P, 2])
        hid, sg = sb("hid", [P, FF]), sb("sg", [P, FF])
        hdh, hdl = sb("hdh", [P, FC, P], F32R), sb("hdl", [P, FC, P], F32R)
        ssa, ssc = sb("ssa", [P, TILES + 1]), sb("ssc", [P, TILES + 7])
        ra, rc = sb("ra", [P, TILES]), sb("rc", [P, TILES])
        st, mv, rs = sb("st", [P, 2, 6]), sb("mv", [P, 2]), sb("rs", [P, 4])
        vd, drop = sb("vd", [P, TILES]), sb("drop", [P, TILES, TOPK])
        tokid, base = sb("tokid", [P, TILES], I32), sb("base", [P, NE])
        rbias, sc, sel = sb("rbias", [P, NE]), sb("sc", [P, NE]), sb("sel", [P, NE])
        gm, gp, gr = sb("gm", [P, NG, 8]), sb("gp", [P, NG + TOPG]), sb("gr", [P, NG + TOPG])
        pen, g8, s8, d8 = sb("pen", [P, NG]), sb("g8", [P, 8]), sb("s8", [P, 8]), sb("d8", [P, 8])
        sp_, sr = sb("selp", [P, NE + 2]), sb("sr", [P, NE + 2])
        mk, gt, dd, junk = sb("mk", [P, NE]), sb("gt", [P, NE]), sb("dd", [P, NE]), sb("junk", [P, TOPK, NE])
        gsum, g6 = sb("gsum", [P, 2]), sb("g6", [P, TOPK])
        mkb, macc = sb("mkb", [P, NE], BF16), sb("macc", [P, NE], BF16)
        trif, trib, oneb = sb("trif", [P, P]), sb("trib", [P, P], BF16), sb("oneb", [P, P], BF16)
        dest, pay = sb("dest", [P, TOPK], I32), sb("pay", [P, TOPK, 2], I32)
        thr, nidx, ecol = sb("thr", [NE, 8]), sb("nidx", [NE, OVMAX]), sb("ecol", [NE, 3])
        oc = sb("oc", [NE, 4]); oi, oq, oj = sb("oi", [NE, OVMAX]), sb("oq", [NE, OVMAX]), sb("oj", [NE, 8])

        psA, psC = ps("psA", [P, D]), ps("psC", [P, D])
        psT = ps("psT", [P, D])
        psU, psR = ps("psU", [P, 2 * FF]), ps("psR", [P, 512])

        names = ("const", "passed", "sums", "zero", "cat_loaded", "x_loaded", "cat_hi", "cat_lo", "wo", "wo_act", "wo_read", "var", "std",
                 "rstd", "norm", "h", "h_stored", "hT", "hT_hi", "hT_lo", "router", "router_copied", "logit", "score", "gu", "sig", "hid",
                 "hidT", "hid_hi", "hid_lo", "down", "acc", "acc_stored", "mask", "rank", "rank_read", "pay", "scat",
                 "init", "gscaled", "gscale", "ovA", "ovB", "ovC", "ovD", "ovE", "ovF")
        S = {n: sem(n) for n in names}
        pieces = [(io["w_out"][:, k:k + 2], woh[:, k:k + 2, :], wol[:, k:k + 2, :]) for k in range(0, KC, 2)]
        for j, w in enumerate(("ws_gate", "ws_up")):
            pieces.append((io[w], guh[:, :, j * FF:(j + 1) * FF], gul[:, :, j * FF:(j + 1) * FF]))
        pieces += [(io["router_w"], rw[:, :, 0:NE], rw[:, :, NE:2 * NE]), (io["ws_down"], dnh[:], dnl[:])]
        N_WO = KC // 2
        w_sp, w_act, w_dve, s_w, n_w = split_weights(nc, ph, pieces, raw)
        consts = [(ident[:], io["ident"]), (lg[:], io["ln1_g"].partition_broadcast(P)),
                  (lb[:], io["ln1_b"].partition_broadcast(P)), (ssa[:], io["ssA"]), (ssc[:], io["ssC"]),
                  (vd[:], io["valid"]), (drop[:], io["drop"]), (tokid[:], io["tokid"]), (base[:], io["base"]),
                  (rbias[:], io["router_bias"].partition_broadcast(P)), (trif[:], io["tri"]),
                  (thr[:], io["thr"]), (nidx[:], io["nidx"]), (ecol[:], io["ecol"])]
        CONST = 16 * len(consts)
        LAST = TILES - 1

        def steps(eng, step):
            step(0, 0, True, True, True)
            with eng.Fori(0, (LAST - 2) // 2) as j:
                step(2 * j + 1, 1, False, True, True)
                step(2 * j + 2, 0, False, True, True)
            step(LAST - 1, 1, False, False, True)
            step(LAST, 0, False, False, False)

        block = ctx.enter_context(nc.Block())

        @block.sync
        def _(sp):
            def load_cat(i):
                sp.wait_ge(S["cat_lo"], i)
                sp.dma_start(cr[:, 0:GQ], io["catA"][bass.ds(i + 1, 1)].rearrange("o p k t -> (o p) k t")).then_inc(S["cat_loaded"], 16)
                sp.dma_start(cr[:, GQ:KC], io["catC"][bass.ds(i + 4, 1)].rearrange("o p k t -> (o p) k t")).then_inc(S["cat_loaded"], 16)

            def load_x(i):
                sp.wait_ge(S["norm"], i)
                sp.dma_start(xr[:], io["x_rows"][bass.ds(i * P, P)]).then_inc(S["x_loaded"], 16)

            load_cat(0)
            load_x(0)
            w_sp(sp, 0, N_WO)
            load_cat(1)
            w_sp(sp, N_WO)
            sp.dma_start(io["table"][0:DROP_SLOT], io["table0"]).then_inc(S["init"], 16)
            sp.wait_ge(S["zero"], 1)
            sp.dma_start(io["h_d"][TPAD:ROWS], acc[:]).then_inc(S["init"], 16)
            sp.dma_start(io["acc_d"][TPAD:ROWS], acc[:]).then_inc(S["init"], 16)

            def step(i, k, first, pre, front):
                if front:
                    load_x(i + 1)
                if pre:
                    load_cat(i + 2)
                if not first:
                    sp.wait_ge(S["acc"], i)
                    sp.dma_start(io["acc_d"][bass.ds((i - 1) * P, P)], acc[:]).then_inc(S["acc_stored"], 16)

            steps(sp, step)
            sp.wait_ge(S["acc"], TILES)
            sp.dma_start(io["acc_d"][bass.ds(LAST * P, P)], acc[:]).then_inc(S["acc_stored"], 16)
            sp.wait_ge(S["acc_stored"], 16 * TILES)
            sp.wait_ge(S["ovF"], 1)

        @block.gpsimd
        def _(pool):
            for dst, src in consts:
                pool.dma_start(dst, src).then_inc(S["const"], 16)
            pool.wait_ge(S["const"], CONST)

            def gain(i, k):
                pool.wait_ge(S["norm"], i + 1)
                nc.gpsimd.tensor_tensor(h[:, k, :], h[:, k, :], lg[:], ALU.mult).then_inc(S["gscaled"], 1)
                pool.wait_ge(S["gscaled"], i + 1)
                nc.gpsimd.tensor_tensor(h[:, k, :], h[:, k, :], lb[:], ALU.add).then_inc(S["h"], 1)
                hold(pool, S["h"], i + 1, S["passed"])
                hold(pool, S["h_stored"], 16 * i, S["passed"])
                pool.dma_start(io["h_d"][bass.ds(i * P, P)], h[:, k, :]).then_inc(S["h_stored"], 16)

            def step(i, k, first, pre, front):
                if front:
                    gain(i + 1, 1 - k)
                if not first:
                    scatter(i - 1)

            def scatter(i):
                hold(pool, S["pay"], i + 1, S["passed"])
                for j in range(TOPK):
                    nc.gpsimd.indirect_dma_start(
                        out=io["table"], out_offset=bass.IndirectOffsetOnAxis(ap=dest[:, j:j + 1].bitcast(U32), axis=0),
                        in_=pay[:, j, :], in_offset=None).then_inc(S["scat"], 16)

            gain(0, 0)
            pool.wait_ge(S["init"], 48)
            steps(pool, step)
            scatter(LAST)
            pool.wait_ge(S["scat"], 16 * TOPK * TILES)
            pool.wait_ge(S["h_stored"], 16 * TILES)

        @block.scalar
        def _(act):
            def round_cat(i):
                act.wait_ge(S["cat_loaded"], 32 * (i + 1))
                act.wait_ge(S["wo"], i)
                nc.scalar.activation(ch[:], cr[:], ACT.Copy).then_inc(S["cat_hi"], 1)

            def scale_attention(i):
                act.wait_ge(S["wo"], i + 1)
                nc.scalar.activation(t[:], psA[:], ACT.Copy, scale=ra[:, bass.ds(i, 1)]).then_inc(S["wo_act"], 1)

            def norm(i, k, fresh):
                act.wait_ge(S["var"], i + 1)
                nc.scalar.activation(rs[:, 1:2], rs[:, 0:1], ACT.Sqrt).then_inc(S["std"], 1)
                act.wait_ge(S["rstd"], i + 1)
                if not fresh:
                    act.wait_ge(S["hT"], i - 1)
                    act.wait_ge(S["acc"], i - 1)
                    act.wait_ge(S["h_stored"], 16 * (i - 1))
                nc.scalar.activation(h[:, k, :], t[:], ACT.Identity, scale=rs[:, 2:3], bias=rs[:, 3:4]).then_inc(S["norm"], 1)

            round_cat(0)
            w_act(act, 0, N_WO)
            act.wait_ge(S["sums"], 1)
            nc.scalar.activation(ra[:], ra[:], ACT.Sqrt)
            nc.scalar.activation(rc[:], rc[:], ACT.Sqrt).then_inc(S["sums"], 1)
            act.wait_ge(S["sums"], 3)
            scale_attention(0)
            round_cat(1)
            norm(0, 0, True)
            w_act(act, N_WO)

            def hidden(i):
                act.wait_ge(S["hidT"], i + 1)
                act.wait_ge(S["down"], i)
                nc.scalar.activation(hdh[:].rearrange("p f t -> p (f t)"), psR[:, 128:384], ACT.Copy).then_inc(S["hid_hi"], 1)

            def step(i, k, first, pre, front):
                if not first:
                    hidden(i - 1)
                act.wait_ge(S["hT"], i + 1)
                act.wait_ge(S["gu"], i)
                nc.scalar.activation(hT[:, :, 0, :], psT[:].rearrange("p (k t) -> p k t", k=KC), ACT.Copy).then_inc(S["hT_hi"], 1)
                if front:
                    scale_attention(i + 1)
                if pre:
                    round_cat(i + 2)
                act.wait_ge(S["router"], i + 1)
                nc.scalar.activation(lt[:], psR[:, 128:384], ACT.Copy).then_inc(S["router_copied"], 1)
                if front:
                    norm(i + 1, 1 - k, first)
                act.wait_ge(S["logit"], i + 1)
                act.wait_ge(S["gscale"], i)
                nc.scalar.activation(sc[:], psR[:, 0:NE], ACT.Sigmoid).then_inc(S["score"], 1)
                act.wait_ge(S["gu"], i + 1)
                act.wait_ge(S["hid"], i)
                nc.scalar.activation(sg[:], psU[:, 0:FF], ACT.Sigmoid).then_inc(S["sig"], 1)

            steps(act, step)
            hidden(LAST)

        @block.vector
        def _(dve):
            V = nc.vector

            def split_cat(i):
                dve.wait_ge(S["cat_hi"], i + 1)
                V.tensor_tensor(cl[:], cr[:], ch[:].bitcast(F32), ALU.subtract).then_inc(S["cat_lo"], 1)

            def residual(i):
                dve.wait_ge(S["wo_act"], i + 1)
                V.scalar_tensor_tensor(t[:], psC[:], rc[:, bass.ds(i, 1)], t[:], ALU.mult, ALU.add).then_inc(S["wo_read"], 1)
                dve.wait_ge(S["wo_read"], i + 1)
                dve.wait_ge(S["x_loaded"], 16 * (i + 1))
                V.scalar_tensor_tensor(t[:], xr[:], ALPHA, t[:], ALU.mult, ALU.add)
                dve.drain()
                for a in range(2):
                    V.bn_stats(st[:, a, :], t[:, a * 512:(a + 1) * 512])
                dve.drain()
                V.bn_aggr(mv[:], st[:])
                dve.drain()
                V.tensor_scalar(rs[:, 0:1], mv[:, 1:2], LN_EPS, None, ALU.add).then_inc(S["var"], 1)

            def scales(i):
                dve.wait_ge(S["std"], i + 1)
                V.reciprocal(rs[:, 2:3], rs[:, 1:2])
                dve.drain()
                V.scalar_tensor_tensor(rs[:, 3:4], mv[:, 0:1], -1.0, rs[:, 2:3], ALU.mult, ALU.mult).then_inc(S["rstd"], 1)

            def hidden(i):
                dve.wait_ge(S["hid_hi"], i + 1)
                V.tensor_tensor(hdl[:].rearrange("p f t -> p (f t)"), psR[:, 128:384],
                                hdh[:].bitcast(F32).rearrange("p f t -> p (f t)"), ALU.subtract).then_inc(S["hid_lo"], 1)

            def accumulate(i, k):
                dve.wait_ge(S["down"], i + 1)
                dve.wait_ge(S["acc_stored"], 16 * i)
                V.scalar_tensor_tensor(acc[:], h[:, k, :], ALPHA, psT[:], ALU.mult, ALU.add).then_inc(S["acc"], 1)

            def pick(i):
                dve.wait_ge(S["score"], i + 1)
                V.tensor_tensor(sel[:], sc[:], rbias[:], ALU.add)
                dve.drain()
                for g in range(NG):
                    V.max(gm[:, g, :], sel[:, g * EPG:(g + 1) * EPG])
                dve.drain()
                V.tensor_tensor(gp[:, 0:NG], gm[:, :, 0], gm[:, :, 1], ALU.add)
                dve.drain()
                V.max(g8[:], gp[:])
                dve.drain()
                V.match_replace(gr[:], g8[:], gp[:], -BIG)
                dve.drain()
                V.tensor_scalar(pen[:], gr[:, 0:NG], -BIG, NEG, ALU.not_equal, ALU.mult)
                dve.drain()
                V.tensor_tensor(sp_[:, 0:NE].rearrange("p (g e) -> p g e", g=NG), sel[:].rearrange("p (g e) -> p g e", g=NG),
                                pen[:].unsqueeze(2).to_broadcast([P, NG, EPG]), ALU.add)
                dve.drain()
                V.max(s8[:], sp_[:])
                dve.drain()
                V.match_replace(sr[:], s8[:], sp_[:], -BIG)
                dve.drain()
                V.tensor_scalar(mk[:], sr[:, 0:NE], -BIG, None, ALU.is_equal)
                V.tensor_scalar(mkb[:], sr[:, 0:NE], -BIG, vd[:, bass.ds(i, 1)], ALU.is_equal, ALU.mult).then_inc(S["mask"], 1)
                dve.drain()
                V.scalar_tensor_tensor(gt[:], sc[:], 1.0, mk[:], ALU.mult, ALU.mult, accum_out=gsum[:, 0:1])
                dve.drain()
                V.reciprocal(gsum[:, 1:2], gsum[:, 0:1])
                dve.drain()
                V.tensor_scalar(gt[:], gt[:], gsum[:, 1:2], 2.5, ALU.mult, ALU.mult).then_inc(S["gscale"], 1)

            def ranks(i):
                dve.wait_ge(S["gscale"], i + 1)
                dve.wait_ge(S["rank"], i + 1)
                V.tensor_tensor(dd[:], psR[:, NE:2 * NE], base[:], ALU.add).then_inc(S["rank_read"], 1)
                V.tensor_tensor(macc[:], macc[:], mkb[:], ALU.add)
                dve.drain()

            def place(i):
                V.tensor_tensor(dd[:], dd[:], mkb[:], ALU.mult)
                dve.drain()
                V.max(d8[:], dd[:])
                dve.drain()
                for j in range(TOPK):
                    V.scalar_tensor_tensor(junk[:, j], dd[:], d8[:, j:j + 1], gt[:], ALU.is_equal, ALU.mult,
                                           accum_out=g6[:, j:j + 1])
                dve.wait_ge(S["scat"], 16 * TOPK * i)
                V.scalar_tensor_tensor(dest[:], d8[:, 0:TOPK], -1.0, drop[:, bass.ds(i, 1), :].rearrange("p o j -> p (o j)"),
                                       ALU.add, ALU.add)
                V.tensor_copy(pay[:, :, 0], tokid[:, bass.ds(i, 1)].to_broadcast([P, TOPK]))
                dve.drain()
                V.tensor_copy(pay[:, :, 1].bitcast(F32), g6[:])
                dve.drain().then_inc(S["pay"], 1)

            V.memset(acc[:], 0.0).then_inc(S["zero"], 1)
            V.memset(ones[:], 1.0)
            V.memset(oneb[:], 1.0)
            V.memset(macc[:], 0.0)
            V.memset(gp[:], BIG)
            V.memset(sp_[:], BIG)
            split_cat(0)
            w_dve(dve, 0, N_WO)
            dve.wait_ge(S["const"], CONST)
            V.tensor_copy(trib[:], trif[:])
            V.tensor_tensor(eye2[:], ident[:, 0:NE], ident[:, NE:2 * NE], ALU.add)
            dve.drain().then_inc(S["zero"], 1)
            V.tensor_scalar(ra[:], ssa[:, 1:TILES + 1], 1.0 / AW, RMS_EPS, ALU.mult, ALU.add)
            V.tensor_scalar(rc[:], ssc[:, 4:4 + TILES], 1.0 / CH, RMS_EPS, ALU.mult, ALU.add).then_inc(S["sums"], 1)
            dve.wait_ge(S["sums"], 2)
            V.reciprocal(ra[:], ra[:])
            V.reciprocal(rc[:], rc[:]).then_inc(S["sums"], 1)
            dve.wait_ge(S["sums"], 3)
            residual(0)
            scales(0)
            split_cat(1)
            w_dve(dve, N_WO)
            dve.wait_ge(S["init"], 48)

            def step(i, k, first, pre, front):
                if not first:
                    hidden(i - 1)
                dve.wait_ge(S["hT_hi"], i + 1)
                V.tensor_tensor(hT[:, :, 1, :], psT[:].rearrange("p (k t) -> p k t", k=KC), hT[:, :, 0, :].bitcast(F32),
                                ALU.subtract).then_inc(S["hT_lo"], 1)
                if not first:
                    ranks(i - 1)
                if front:
                    residual(i + 1)
                if pre:
                    split_cat(i + 2)
                if front:
                    scales(i + 1)
                if not first:
                    accumulate(i - 1, 1 - k)
                    place(i - 1)
                dve.wait_ge(S["sig"], i + 1)
                V.tensor_tensor(hid[:], psU[:, 0:FF], sg[:], ALU.mult)
                dve.drain()
                V.tensor_tensor(hid[:], hid[:], psU[:, FF:2 * FF], ALU.mult).then_inc(S["hid"], 1)
                pick(i)

            steps(dve, step)
            hidden(LAST)
            ranks(LAST)
            place(LAST)
            accumulate(LAST, 0)

            dve.wait_ge(S["ovA"], 1)
            V.tensor_copy(oc[:, 0:1], psR[0:NE, 0:1])
            dve.drain()
            V.tensor_scalar(oj[:], thr[:], oc[:, 0:1], None, ALU.is_lt)
            dve.drain()
            V.tensor_reduce(oc[:, 1:2], oj[:], AX_X, ALU.add)
            dve.drain().then_inc(S["ovB"], 1)
            dve.wait_ge(S["ovC"], 1)
            V.tensor_copy(oc[:, 2:3], psR[0:NE, 1:2])
            dve.drain()
            V.tensor_tensor(oc[:, 3:4], oc[:, 2:3], oc[:, 1:2], ALU.add)
            dve.drain()
            V.tensor_scalar(oi[:], nidx[:], oc[:, 2:3], None, ALU.is_ge)
            dve.drain()
            V.scalar_tensor_tensor(oi[:], nidx[:], oc[:, 3:4], oi[:], ALU.is_lt, ALU.mult)
            dve.drain()
            V.scalar_tensor_tensor(oq[:], nidx[:], oc[:, 2:3], oi[:], ALU.subtract, ALU.mult)
            dve.drain().then_inc(S["ovD"], 1)
            dve.wait_ge(S["ovE"], 1)
            V.tensor_copy(ov[:, 0:OVMAX], psR[0:1, 64:64 + OVMAX])
            V.tensor_scalar(ov[:, OVMAX:2 * OVMAX], psR[0:1, 128:128 + OVMAX], float(TRASH_SLOT), None, ALU.add)
            V.tensor_scalar(oj[0:1, 0:1], psR[0:1, 192:193], 1.0, None, ALU.mult)
            dve.drain()
            V.tensor_scalar(oq[0:1, 0:OVP], nidx[0:1, 0:OVMAX:2], oj[0:1, 0:1], None, ALU.is_lt)
            dve.drain()
            V.tensor_reduce(oj[0:1, 1:2], oq[0:1, 0:OVP], AX_X, ALU.add)
            dve.drain()
            V.tensor_copy(ov[:, 2 * OVMAX:2 * OVMAX + 1], oj[0:1, 1:2])
            dve.drain().then_inc(S["ovF"], 1)

        @block.tensor
        def _(pe):
            pe.wait_ge(s_w, N_WO // 2)

            def three(out, lh, ll, rh, rl, start, stop):
                nc.tensor.matmul(out, lh, rh, start=start, stop=False)
                nc.tensor.matmul(out, lh, rl, start=False, stop=False)
                return nc.tensor.matmul(out, ll, rh, start=False, stop=stop)

            def project(i, part):
                if part == 0:
                    pe.wait_ge(S["cat_lo"], i + 1)
                    pe.wait_ge(S["wo_read"], i)
                c0, c1, out = ((0, GQ, psA), (GQ, KC, psC))[part]
                for hf in range(2):
                    cols = slice(hf * 512, (hf + 1) * 512)
                    for c in range(c0, c1):
                        last = three(out[:, cols], ch[:, c, :], cl[:, c, :], woh[:, c, cols], wol[:, c, cols],
                                     c == c0, c == c1 - 1)
                if part == 1:
                    last.then_inc(S["wo"], 1)

            def rank(i):
                pe.wait_ge(S["mask"], i + 1)
                pe.wait_ge(S["pay"], i)
                pe.wait_ge(S["hid_lo"], i + 1)
                nc.tensor.matmul(psR[:, NE:2 * NE], trib[:], mkb[:], start=True, stop=False)
                nc.tensor.matmul(psR[:, NE:2 * NE], oneb[:], macc[:], start=False, stop=True).then_inc(S["rank"], 1)

            def hidden_T(i):
                pe.wait_ge(S["hid"], i + 1)
                pe.wait_ge(S["score"], i + 1)
                pe.wait_ge(S["hid_lo"], i)
                for f in range(FC):
                    last = nc.tensor.transpose(psR[:, 128 + f * P:128 + (f + 1) * P], hid[:, f * P:(f + 1) * P], ident[:])
                last.then_inc(S["hidT"], 1)

            def down(i):
                pe.wait_ge(S["hid_lo"], i + 1)
                for hf in range(2):
                    cols = slice(hf * 512, (hf + 1) * 512)
                    for f in range(FC):
                        last = three(psT[:, cols], hdh[:, f, :], hdl[:, f, :], dnh[:, f, cols], dnl[:, f, cols],
                                     f == 0, f == FC - 1)
                last.then_inc(S["down"], 1)

            project(0, 0)
            pe.wait_ge(s_w, N_WO)
            project(0, 1)
            pe.wait_ge(S["zero"], 2)

            def step(i, k, first, pre, front):
                if front:
                    project(i + 1, 0)
                if not first:
                    hidden_T(i - 1)
                pe.wait_ge(S["h"], i + 1)
                if not first:
                    pe.wait_ge(S["acc"], i - 1)
                for kc in range(KC):
                    last = nc.tensor.transpose(psT[:, kc * P:(kc + 1) * P], h[:, k, kc * P:(kc + 1) * P], ident[:])
                last.then_inc(S["hT"], 1)
                if front:
                    project(i + 1, 1)
                if not first:
                    rank(i - 1)
                pe.wait_ge(S["hT_lo"], i + 1)
                if not first:
                    down(i - 1)
                if first:
                    pe.wait_ge(s_w, n_w)
                pe.wait_ge(S["rank_read"], i)
                pe.wait_ge(S["hid"], i)
                for kc in range(KC):
                    last = nc.tensor.matmul(psR[:, 128:384], rw[:, kc, :], hT[:, kc].rearrange("p s t -> p (s t)"),
                                            start=(kc == 0), stop=(kc == KC - 1))
                last.then_inc(S["router"], 1)
                for kc in range(KC):
                    last = three(psU[:], hT[:, kc, 0, :], hT[:, kc, 1, :], guh[:, kc, :], gul[:, kc, :], kc == 0, kc == KC - 1)
                last.then_inc(S["gu"], 1)
                pe.wait_ge(S["router_copied"], i + 1)
                for part in range(2):
                    last = nc.tensor.matmul(psR[:, 0:NE], lt[:, part * P:(part + 1) * P], eye2[:], start=(part == 0), stop=(part == 1))
                last.then_inc(S["logit"], 1)

            steps(pe, step)
            hidden_T(LAST)
            rank(LAST)
            down(LAST)
            pe.wait_ge(S["pay"], TILES)
            pe.wait_ge(S["hid_lo"], TILES)
            nc.tensor.matmul(psR[0:NE, 0:1], macc[:], oneb[:, 0:1], start=True, stop=True).then_inc(S["ovA"], 1)
            pe.wait_ge(S["ovB"], 1)
            nc.tensor.matmul(psR[0:NE, 1:2], trif[0:NE, 0:NE], oc[:, 1:2], start=True, stop=True).then_inc(S["ovC"], 1)
            pe.wait_ge(S["ovD"], 1)
            nc.tensor.matmul(psR[0:1, 64:64 + OVMAX], ecol[:, 0:1], oi[:], start=True, stop=True)
            nc.tensor.matmul(psR[0:1, 128:128 + OVMAX], ecol[:, 1:2], oi[:], start=True, stop=False)
            nc.tensor.matmul(psR[0:1, 128:128 + OVMAX], ecol[:, 2:3], oq[:], start=False, stop=True)
            nc.tensor.matmul(psR[0:1, 192:193], oc[:, 1:2], ones[0:NE, 0:1], start=True, stop=True).then_inc(S["ovE"], 1)


def stage_experts(nc, io, ov):
    PAIRS = NE // 2
    with ExitStack() as ctx:
        ph = Phase(nc, ctx, "ex")
        sb, ps, sem = ph.sb, ph.ps, ph.sem
        raw = sb("raw", [P, 2, 3, 2048])
        guh, gul = sb("guh", [P, 2, KC, 2 * FF], F32R), sb("gul", [P, 2, KC, 2 * FF], F32R)
        dnh, dnl = sb("dnh", [P, 2, FC, D], F32R), sb("dnl", [P, 2, FC, D], F32R)
        xg = sb("xg", [P, 4, D])
        xh, xl = sb("xh", [P, 2, KC, P], F32R), sb("xl", [P, 2, KC, P], F32R)
        sg, hid = sb("sg", [P, FF]), sb("hid", [P, 2, FF])
        hdh, hdl = sb("hdh", [P, FC, P], F32R), sb("hdl", [P, FC, P], F32R)
        y = sb("y", [P, 4, D])
        ent = sb("ent", [P, 4, 2], I32)
        use = sb("use", [P, 4, 2], I32)
        ident = sb("ident", [P, P])
        psX, psU = ps("psX", [P, D]), ps("psU", [P, 2, 2 * FF])
        psH, psY = ps("psH", [P, FC * P]), ps("psY", [P, D])

        s_const, s_passed, s_sp_passed = sem("const"), sem("passed"), sem("sp_passed")
        s_w = [[sem(f"{n}_loaded{b}") for n in ("gate", "up", "down")] for b in range(2)]
        s_round, s_split = sem("rounded"), sem("split")
        s_ent = [sem(f"entries{b}") for b in range(2)]
        s_row = [sem(f"rows{k}") for k in range(4)]
        s_use, s_add, s_y = sem("entries_kept"), sem("added"), sem("y")
        s_xT, s_xh, s_xl = sem("xT"), sem("xT_hi"), sem("xT_lo")
        s_gu, s_sig, s_hid = sem("gate_up"), sem("sig"), sem("hid")
        s_hT, s_hh, s_hl, s_dn = sem("hidT"), sem("hidT_hi"), sem("hidT_lo"), sem("down")

        PIECES = [(b, kind, part) for b in range(2) for kind in (0, 1, 2) for part in range(2)]
        STEP_PIECES = (range(0, 4), range(4, 7), range(7, 10), range(10, 12))
        EARLY = (4, 1, 3, 1)

        def piece(n):
            b, kind, part = PIECES[n]
            src = raw[:, b, kind, part * 1024:(part + 1) * 1024]
            if kind < 2:
                k0 = part * KC // 2
                at = (slice(None), b, slice(k0, k0 + KC // 2), slice(kind * FF, (kind + 1) * FF))
                return src.rearrange("p (k f) -> p k f", f=FF), guh[at], gul[at]
            return src, dnh[:, b, part, :], dnl[:, b, part, :]

        def pairs(eng, pair):
            pair(0, True, None)
            with eng.Fori(1, PAIRS) as p:
                pair(p, False, None)
            more = eng.value_load(ov[0:1, 2 * OVMAX:2 * OVMAX + 1], min_val=0, max_val=OVP)
            with eng.If(more > 0):
                with eng.Fori(0, OVP) as j:
                    with eng.If(more > j):
                        pair(PAIRS + j, False, j)
            return PAIRS + more

        block = ctx.enter_context(nc.Block())

        @block.sync
        def _(sp):
            sp.dma_start(ident[:], io["ident"]).then_inc(s_const, 16)

            def pair(p, first, j):
                for b in range(2):
                    if j is None:
                        e = 2 * p + b
                        slot = e * SLOTS
                    else:
                        e = sp.value_load(ov[0:1, bass.ds(2 * j + b, 1)], min_val=0, max_val=NE - 1)
                        slot = sp.value_load(ov[0:1, bass.ds(2 * j + b + OVMAX, 1)], min_val=0, max_val=TRASH_SLOT)
                    if not first:
                        hold(sp, s_use, 4 * p + 2 * b - 2, s_sp_passed)
                        hold(sp, s_row[2 * b], 16 * p, s_sp_passed)
                        hold(sp, s_row[2 * b + 1], 16 * p, s_sp_passed)
                    sp.dma_start(ent[:, 2 * b:2 * b + 2, :],
                                 io["table"][bass.ds(slot, BLK)].rearrange("(t p) c -> p t c", p=P)).then_inc(s_ent[b], 16)
                    if not first:
                        hold(sp, s_split, 12 * p + 6 * b - 6, s_sp_passed)
                    for kind, name in enumerate(("w_gate", "w_up", "w_down")):
                        if first and b == 0 and kind == 2:
                            hold(sp, s_row[0], 16, s_sp_passed)
                            hold(sp, s_row[1], 16, s_sp_passed)
                        w = io[name][bass.ds(e, 1)].rearrange("o (k p) n -> (o p) k n", p=P)
                        sp.dma_start(raw[:, b, kind].rearrange("p (k n) -> p k n", n=w.shape[2]), w).then_inc(s_w[b][kind], 16)

            pairs(sp, pair)

        @block.gpsimd
        def _(pool):
            def add_rows(n, k):
                hold(pool, s_y, n + 1, s_passed)
                nc.gpsimd.indirect_dma_start(
                    out=io["acc_d"], out_offset=bass.IndirectOffsetOnAxis(ap=use[:, k, 0:1].bitcast(U32), axis=0),
                    in_=y[:, k, :], in_offset=None, compute_op=ALU.add).then_inc(s_add, 16)
                hold(pool, s_add, 16 * (n + 1), s_passed)

            def pair(p, first, j):
                for k in range(4):
                    n = 4 * p + k
                    if k % 2 == 0:
                        hold(pool, s_ent[k // 2], 16 * (p + 1), s_passed)
                    if not first:
                        hold(pool, s_xT, n - 3, s_passed)
                    nc.gpsimd.indirect_dma_start(
                        out=xg[:, k, :], out_offset=None, in_=io["h_d"],
                        in_offset=bass.IndirectOffsetOnAxis(ap=ent[:, k, 0:1].bitcast(U32), axis=0)).then_inc(s_row[k], 16)
                    if not first:
                        add_rows(n - 4, k)
                    nc.gpsimd.tensor_copy(use[:, k, :], ent[:, k, :]).then_inc(s_use, 1)
                    hold(pool, s_use, n + 1, s_passed)

            end = pairs(pool, pair)
            for k in range(4):
                add_rows(4 * end - 4 + k, k)

        def step_parts(first, k):
            return not (first and k < 1), not (first and k < 2)

        @block.scalar
        def _(act):
            A = nc.scalar

            def hidden(m):
                act.wait_ge(s_hT, m + 1)
                act.wait_ge(s_dn, m)
                A.activation(hdh[:].rearrange("p f t -> p (f t)"), psH[:], ACT.Copy).then_inc(s_hh, 1)

            def sigmoid(m, k):
                act.wait_ge(s_gu, m + 1)
                act.wait_ge(s_hid, m)
                A.activation(sg[:], psU[:, k % 2, 0:FF], ACT.Sigmoid).then_inc(s_sig, 1)

            def output(m, k, fresh):
                act.wait_ge(s_dn, m + 1)
                if not fresh:
                    act.wait_ge(s_add, 16 * (m - 2))
                A.activation(y[:, k % 4, :], psY[:], ACT.Copy).then_inc(s_y, 1)

            def split(p, first, k, part):
                for q in (STEP_PIECES[k][:EARLY[k]] if part == 0 else STEP_PIECES[k][EARLY[k]:]):
                    b, kind, half_ = PIECES[q]
                    act.wait_ge(s_w[b][kind], 16 * (p + 1))
                    if q in (0, 6) and not first:
                        act.wait_ge(s_gu, 4 * p - 2 + 2 * b)
                    if q in (4, 10) and not first:
                        act.wait_ge(s_dn, 4 * p - 2 + 2 * b)
                    src, hi, lo = piece(q)
                    A.activation(hi, src, ACT.Copy).then_inc(s_round, 1)

            def pair(p, first, j):
                for k in range(4):
                    n = 4 * p + k
                    has1, has2 = step_parts(first, k)
                    if has2:
                        hidden(n - 2)
                    split(p, first, k, 0)
                    if has1:
                        sigmoid(n - 1, k - 1)
                    act.wait_ge(s_xT, n + 1)
                    if not (first and k < 2):
                        act.wait_ge(s_gu, n - 1)
                    A.activation(xh[:, k % 2].rearrange("p k t -> p (k t)"), psX[:], ACT.Copy).then_inc(s_xh, 1)
                    split(p, first, k, 1)
                    if has2:
                        output(n - 2, k - 2, first)

            end = pairs(act, pair)
            n = 4 * end
            hidden(n - 2)
            sigmoid(n - 1, 3)
            output(n - 2, 2, False)
            hidden(n - 1)
            output(n - 1, 3, False)

        @block.vector
        def _(dve):
            V = nc.vector

            def hidden(m):
                dve.wait_ge(s_hh, m + 1)
                V.tensor_tensor(hdl[:].rearrange("p f t -> p (f t)"), psH[:],
                                hdh[:].bitcast(F32).rearrange("p f t -> p (f t)"), ALU.subtract).then_inc(s_hl, 1)

            def activate(m, k):
                dve.wait_ge(s_sig, m + 1)
                dve.wait_ge(s_use, m + 1)
                if not isinstance(m, int) or m >= 2:
                    dve.wait_ge(s_hT, m - 1)
                gate = use[:, k % 4, 1:2].bitcast(F32)
                V.scalar_tensor_tensor(hid[:, k % 2, :], psU[:, k % 2, 0:FF], gate, sg[:], ALU.mult, ALU.mult)
                dve.drain()
                V.tensor_tensor(hid[:, k % 2, :], hid[:, k % 2, :], psU[:, k % 2, FF:2 * FF], ALU.mult).then_inc(s_hid, 1)

            def split(p, first, k, part):
                for q in (STEP_PIECES[k][:EARLY[k]] if part == 0 else STEP_PIECES[k][EARLY[k]:]):
                    src, hi, lo = piece(q)
                    dve.wait_ge(s_round, 12 * p + q + 1)
                    V.tensor_tensor(lo, src, hi.bitcast(F32), ALU.subtract).then_inc(s_split, 1)

            def pair(p, first, j):
                for k in range(4):
                    n = 4 * p + k
                    has1, has2 = step_parts(first, k)
                    if has2:
                        hidden(n - 2)
                    split(p, first, k, 0)
                    if has1:
                        activate(n - 1, k - 1)
                    dve.wait_ge(s_xh, n + 1)
                    V.tensor_tensor(xl[:, k % 2].rearrange("p k t -> p (k t)"), psX[:],
                                    xh[:, k % 2].bitcast(F32).rearrange("p k t -> p (k t)"), ALU.subtract).then_inc(s_xl, 1)
                    split(p, first, k, 1)

            end = pairs(dve, pair)
            n = 4 * end
            hidden(n - 2)
            activate(n - 1, 3)
            hidden(n - 1)

        @block.tensor
        def _(pe):
            pe.wait_ge(s_const, 16)

            def three(out, lh, ll, rh, rl, start, stop):
                nc.tensor.matmul(out, lh, rh, start=start, stop=False)
                nc.tensor.matmul(out, lh, rl, start=False, stop=False)
                return nc.tensor.matmul(out, ll, rh, start=False, stop=stop)

            def hidden_T(m, k):
                pe.wait_ge(s_hid, m + 1)
                pe.wait_ge(s_hl, m)
                for f in range(FC):
                    last = nc.tensor.transpose(psH[:, f * P:(f + 1) * P], hid[:, k % 2, f * P:(f + 1) * P], ident[:])
                last.then_inc(s_hT, 1)

            def gate_up(m, k, b, pieces):
                pe.wait_ge(s_split, pieces)
                pe.wait_ge(s_xl, m + 1)
                if not isinstance(m, int) or m >= 1:
                    pe.wait_ge(s_hid, m - 1)
                for kc in range(KC):
                    last = three(psU[:, k % 2, :], xh[:, k % 2, kc, :], xl[:, k % 2, kc, :],
                                 guh[:, b, kc, :], gul[:, b, kc, :], kc == 0, kc == KC - 1)
                last.then_inc(s_gu, 1)

            def down(m, b, pieces):
                pe.wait_ge(s_hl, m + 1)
                pe.wait_ge(s_split, pieces)
                pe.wait_ge(s_y, m)
                for hf in range(2):
                    cols = slice(hf * 512, (hf + 1) * 512)
                    for f in range(FC):
                        last = three(psY[:, cols], hdh[:, f, :], hdl[:, f, :], dnh[:, b, f, cols], dnl[:, b, f, cols],
                                     f == 0, f == FC - 1)
                last.then_inc(s_dn, 1)

            GU_AT, DN_AT = (4, 4, 10, 10), (6, 6, 12, 12)

            def pair(p, first, j):
                for k in range(4):
                    n = 4 * p + k
                    has1, has2 = step_parts(first, k)
                    if has2:
                        hidden_T(n - 2, k - 2)
                    if has1:
                        q = (k - 1) % 4
                        gate_up(n - 1, k - 1, q // 2, 12 * p + GU_AT[q] - (12 if k < 1 else 0))
                    pe.wait_ge(s_row[k], 16 * (p + 1))
                    pe.wait_ge(s_xl, n)
                    for kc in range(KC):
                        last = nc.tensor.transpose(psX[:, kc * P:(kc + 1) * P], xg[:, k, kc * P:(kc + 1) * P], ident[:])
                    last.then_inc(s_xT, 1)
                    if has2:
                        q = (k - 2) % 4
                        down(n - 2, q // 2, 12 * p + DN_AT[q] - (12 if k < 2 else 0))

            end = pairs(pe, pair)
            n = 4 * end
            hidden_T(n - 2, 2)
            gate_up(n - 1, 3, 1, 12 * end - 2)
            down(n - 2, 1, 12 * end)
            hidden_T(n - 1, 3)
            down(n - 1, 1, 12 * end)


def stage_norm(nc, io):
    with ExitStack() as ctx:
        ph = Phase(nc, ctx, "ln")
        sb, sem = ph.sb, ph.sem
        G = 2
        FULL = TILES // G
        t, z = sb("t", [P, 2, G, D]), sb("z", [P, TILES, D])
        lg, lb = sb("lg", [P, D]), sb("lb", [P, D])
        st, mv, rs = sb("st", [P, 2, G, 2, 6]), sb("mv", [P, 2, G, 2]), sb("rs", [P, 2, G, 4])
        s_const, s_var, s_std, s_rstd, s_norm, s_gain, s_out = (sem(n) for n in ("const", "var", "std", "rstd", "norm", "gain", "out"))
        s_t, s_st = [sem(f"loaded{b}") for b in range(2)], sem("stored")
        block = ctx.enter_context(nc.Block())

        def groups(eng, group):
            with eng.Fori(0, FULL // 2) as j:
                group(2 * j, 0, G)
                group(2 * j + 1, 1, G)
            group(FULL, 0, 1)

        def out_tile(g, q):
            return z[:, bass.ds(G * g + q, 1), :].rearrange("p o d -> p (o d)")

        def rows(name, g, n):
            return io[name][bass.ds(g * G * P, n * P)].rearrange("(b p) d -> p b d", p=P)

        @block.sync
        def _(sp):
            for b in range(2):
                sp.dma_start(t[:, b], rows("acc_d", b, G)).then_inc(s_t[b], 16)
            sp.dma_start(lg[:], io["ln2_g"].partition_broadcast(P)).then_inc(s_const, 16)
            sp.dma_start(lb[:], io["ln2_b"].partition_broadcast(P)).then_inc(s_const, 16)

            def store(g, n):
                sp.wait_ge(s_out, G * g + n)
                sp.dma_start(rows("y", g, n), z[:, bass.ds(G * g, n), :]).then_inc(s_st, 16)

            with sp.Fori(0, FULL // 2 - 1) as j:
                for b in range(2):
                    sp.wait_ge(s_norm, (2 * j + b + 1) * G)
                    sp.dma_start(t[:, b], rows("acc_d", 2 * j + 2 + b, G)).then_inc(s_t[b], 16)
                    store(2 * j + b, G)
            sp.wait_ge(s_norm, (FULL - 1) * G)
            sp.dma_start(t[:, 0, 0:1], rows("acc_d", FULL, 1)).then_inc(s_t[0], 16)
            store(FULL - 2, G)
            store(FULL - 1, G)
            store(FULL, 1)
            sp.wait_ge(s_st, 16 * (FULL + 1))

        @block.vector
        def _(dve):
            V = nc.vector

            def stats(g, b, r, n):
                dve.wait_ge(s_t[b], 16 * (r + 1))
                for q in range(n):
                    for a in range(2):
                        V.bn_stats(st[:, b, q, a, :], t[:, b, q, a * 512:(a + 1) * 512])
                dve.drain()
                for q in range(n):
                    V.bn_aggr(mv[:, b, q, :], st[:, b, q])
                dve.drain()
                V.tensor_scalar(rs[:, b, 0:n, 0:1], mv[:, b, 0:n, 1:2], LN_EPS, None, ALU.add).then_inc(s_var, 1)

            def scales(g, b, n):
                dve.wait_ge(s_std, g + 1)
                V.reciprocal(rs[:, b, 0:n, 2:3], rs[:, b, 0:n, 1:2])
                dve.drain()
                V.scalar_tensor_tensor(rs[:, b, 0:n, 3:4], mv[:, b, 0:n, 0:1], -1.0, rs[:, b, 0:n, 2:3],
                                       ALU.mult, ALU.mult).then_inc(s_rstd, 1)

            def shift(g, b, n):
                for q in range(n):
                    dve.wait_ge(s_gain, G * g + q + 1)
                    V.tensor_tensor(out_tile(g, q), out_tile(g, q), lb[:], ALU.add).then_inc(s_out, 1)

            stats(0, 0, 0, G)
            scales(0, 0, G)
            dve.wait_ge(s_const, 32)

            def step(g, b, after, r, n):
                stats(g + 1, after, r, n)
                scales(g + 1, after, n)
                shift(g, b, G)

            with dve.Fori(0, FULL // 2 - 1) as j:
                step(2 * j, 0, 1, j, G)
                step(2 * j + 1, 1, 0, j + 1, G)
            step(FULL - 2, 0, 1, FULL // 2 - 1, G)
            step(FULL - 1, 1, 0, FULL // 2, 1)
            shift(FULL, 0, 1)

        @block.scalar
        def _(act):
            def group(g, b, n):
                act.wait_ge(s_var, g + 1)
                nc.scalar.activation(rs[:, b, 0:n, 1:2], rs[:, b, 0:n, 0:1], ACT.Sqrt).then_inc(s_std, 1)
                act.wait_ge(s_rstd, g + 1)
                for q in range(n):
                    nc.scalar.activation(out_tile(g, q), t[:, b, q, :], ACT.Identity, scale=rs[:, b, q, 2:3],
                                         bias=rs[:, b, q, 3:4]).then_inc(s_norm, 1)

            groups(act, group)

        @block.gpsimd
        def _(pool):
            pool.wait_ge(s_const, 32)

            def gain(g, b, n):
                for q in range(n):
                    pool.wait_ge(s_norm, G * g + q + 1)
                    nc.gpsimd.tensor_tensor(out_tile(g, q), out_tile(g, q), lg[:], ALU.mult).then_inc(s_gain, 1)

            groups(pool, gain)


def build(nc, io):
    ctx = ExitStack()
    with ctx:
        ov = ctx.enter_context(nc.sbuf_tensor("further_blocks", [1, 2 * OVMAX + 1], I32))
        stage_attention(nc, io)
        stage_conv(nc, io)
        stage_dense(nc, io, ov)
        stage_experts(nc, io, ov)
        stage_norm(nc, io)


def kernel(x_prompt, x_sample, cache_k, cache_v, state_conv, w_in, attn_sinks, conv_w, g_attn_out, g_conv_out,
           w_out, ln1_g, ln1_b, router_w, router_bias, w_gate, w_up, w_down, ws_gate, ws_up, ws_down, ln2_g, ln2_b):
    import concourse.bacc as bacc
    from concourse.bass_utils import run_bass_kernel_spmd

    A = lambda a: np.asarray(a)
    C = np.ascontiguousarray
    xs = np.concatenate([A(x_prompt).reshape(SEQ, D), A(x_sample).reshape(NSAMP, D),
                         np.zeros((TPAD - T, D), np.float32)])
    rows = lambda w, n: C(A(w)[0].reshape(n, P, -1).transpose(1, 0, 2))
    sinks = A(attn_sinks)[0]
    srow = C(np.broadcast_to(sinks.reshape(KVH, 1, 1, GQ, 1), (KVH, 2, 4, GQ, DEC_S)).reshape(4, P).T)
    w_out_a = A(w_out)[0][:AW].reshape(KVH, GQ, HD, D).transpose(0, 2, 1, 3).reshape(P, GQ, D)
    w_out_c = A(w_out)[0][AW:].reshape(CC, P, D).transpose(1, 0, 2)
    data = {
        "xT": C(np.concatenate([xs, np.zeros((3 * P, D), np.float32)]).reshape(TILES + 3, P, KC, P).transpose(0, 3, 2, 1)), "x_rows": xs,
        "cache_k": A(cache_k)[0].reshape(DEC_B, P, KVH * HD), "cache_vn": A(cache_v)[0].reshape(DEC_B, P, KVH * HD),
        "cache_kT": C(A(cache_k)[0].reshape(2, 4, P, KVH * HD).transpose(3, 0, 1, 2).reshape(P, 2, 4 * P)),
        "cache_v": C(A(cache_v)[0].reshape(DEC_B, P, KVH * HD).transpose(1, 0, 2)),
        "state_conv": C(A(state_conv)[0].reshape(DEC_B, 2, CC, P).transpose(3, 2, 0, 1)),
        "w_in": rows(w_in, KC), "w_out": C(np.concatenate([w_out_a, w_out_c], 1)),
        "sinks": sinks, "srow": srow, "conv_w": C(A(conv_w)[0].reshape(3, CC, P).transpose(2, 1, 0)),
        "g_attn": C(A(g_attn_out)[0].reshape(KVH, GQ, HD).transpose(0, 2, 1).reshape(P, GQ)),
        "g_conv": C(A(g_conv_out)[0].reshape(CC, P).T),
        "ln1_g": A(ln1_g)[0], "ln1_b": A(ln1_b)[0], "ln2_g": A(ln2_g)[0], "ln2_b": A(ln2_b)[0],
        "router_w": rows(router_w, KC), "router_bias": A(router_bias)[0],
        "w_gate": A(w_gate)[0], "w_up": A(w_up)[0], "w_down": A(w_down)[0],
        "ws_gate": rows(ws_gate, KC), "ws_up": rows(ws_up, KC), "ws_down": rows(ws_down, FC),
    }
    data.update(shape_constants())
    nc = bacc.Bacc("TRN2", target_bir_lowering=False, num_devices=1)
    io, arrays = {}, {}
    for name, a in data.items():
        arrays[name] = C(a)
        io[name] = nc.dram_tensor(name, a.shape, mybir.dt.from_np(a.dtype), kind="ExternalInput").ap()
    outs = {"y": (TPAD, D), "kv_all": (TILES, P, 2, P), "ck_tail": (DEC_B, P - DEC_S, P), "cv_tail": (DEC_B, P - DEC_S, P),
            "conv_p": (P, CC, 2), "conv_s": (P, CC, DEC_B, 2)}
    for name, shape in outs.items():
        io[name] = nc.dram_tensor(name, shape, F32, kind="ExternalOutput").ap()
    inner = {"catA": ((TILES + 1, P, GQ, P), F32), "catC": ((TILES + 4, P, CC, P), F32), "ssA": ((P, TILES + 1), F32),
             "ssC": ((P, TILES + 7), F32), "h_d": ((ROWS, D), F32), "acc_d": ((ROWS, D), F32), "table": ((SLOT_ROWS, 2), I32)}
    for name, (shape, dt) in inner.items():
        io[name] = nc.dram_tensor(name, shape, dt, kind="Internal").ap()
    build(nc, io)
    r = run_bass_kernel_spmd(nc, [arrays], core_ids=[0]).results[0]
    y, kv = r["y"], r["kv_all"]

    def window(n, tail):
        new = kv[TILES - 1, :NSAMP, n].reshape(DEC_B, DEC_S, P)
        return np.concatenate([r[tail], new], 1).reshape(1, DEC_B, P, KVH, HD)

    last = kv[PT_TILES - 1]
    return (y[:SEQ].reshape(1, SEQ, D), y[SEQ:T].reshape(DEC_B, DEC_S, D),
            C(last[:, 0]).reshape(1, 1, P, KVH, HD), C(last[:, 1]).reshape(1, 1, P, KVH, HD),
            C(r["conv_p"].transpose(2, 1, 0)).reshape(1, 1, 2, CH),
            window(0, "ck_tail"), window(1, "cv_tail"),
            C(r["conv_s"].transpose(2, 3, 1, 0)).reshape(1, DEC_B, 2, CH))
```
